# Optimizing a Trainium2 kernel written in Bass

```python
import math
import numpy as np
import jax
import jax.numpy as jnp
from jax import lax

D_MODEL = 1024
BATCH = 1
SEQ = 1024
DEPTH = 1

CHUNK = 64
Q_BLOCK = 128
NORM_EPS = 1e-6
MLA_HEADS = 4
MLA_Q_RANK = 384
MLA_KV_RANK = 256
MLA_NOPE = 128
MLA_ROPE = 64
MLA_V = 128
ROPE_THETA = 10000.0
GDN_HEADS = 4
GDN_DK = 128
GDN_DV = 128
GDN_CONV = 4
GDN_QKV = GDN_HEADS * (2 * GDN_DK + GDN_DV)
MIX_WIDTH = MLA_HEADS * MLA_V + GDN_HEADS * GDN_DV
IN_SPLITS = (MLA_Q_RANK, MLA_KV_RANK, MLA_ROPE, GDN_QKV, GDN_HEADS * GDN_DV, GDN_HEADS, GDN_HEADS)
D_IN = MLA_Q_RANK + MLA_KV_RANK + MLA_ROPE + GDN_QKV + GDN_HEADS * GDN_DV + 2 * GDN_HEADS
N_EXPERTS = 64
N_GROUPS = 8
TOPK_GROUPS = 4
TOP_K = 8
D_EXPERT = 256
D_SHARED = 256
ROUTED_SCALE = 2.5
MOE_BLOCK = 128

kernel_name = 'hybrid_mla_gdn_moe_adaln'

def rms_norm(x, w):
    xf = x.astype(jnp.float32)
    y = xf * lax.rsqrt(jnp.mean(xf * xf, axis=-1, keepdims=True) + NORM_EPS)
    return (y * w.astype(jnp.float32)).astype(x.dtype)

def l2norm(x):
    return x * lax.rsqrt(jnp.sum(x * x, axis=-1, keepdims=True) + 1e-6)

def apply_rope(x, cos, sin):
    x1, x2 = jnp.split(x.astype(jnp.float32), 2, axis=-1)
    return jnp.concatenate([x1 * cos - x2 * sin, x2 * cos + x1 * sin], axis=-1).astype(x.dtype)

def causal_depthwise_conv(x, w):
    K, C = w.shape
    return lax.conv_general_dilated(x, w.reshape(K, 1, C).astype(x.dtype), window_strides=(1,),
                                    padding=((K - 1, 0),), dimension_numbers=('NWC', 'WIO', 'NWC'),
                                    feature_group_count=C)

def mla_group(c_q, c_kv, k_pe, positions, q_a_norm_w, wq_b, kv_a_norm_w, wkv_b):
    B, S, _ = c_q.shape
    q = (rms_norm(c_q, q_a_norm_w) @ wq_b).reshape(B, S, MLA_HEADS, MLA_NOPE + MLA_ROPE)
    q_nope, q_pe = q[..., :MLA_NOPE], q[..., MLA_NOPE:]
    kv = (rms_norm(c_kv, kv_a_norm_w) @ wkv_b).reshape(B, S, MLA_HEADS, MLA_NOPE + MLA_V)
    k_nope, v = kv[..., :MLA_NOPE], kv[..., MLA_NOPE:]
    inv_freq = 1.0 / (ROPE_THETA ** (jnp.arange(0, MLA_ROPE, 2, dtype=jnp.float32) / MLA_ROPE))
    ang = positions.astype(jnp.float32)[..., None] * inv_freq
    cos, sin = jnp.cos(ang), jnp.sin(ang)
    q_pe = apply_rope(q_pe, cos[:, :, None, :], sin[:, :, None, :])
    k_pe = apply_rope(k_pe, cos, sin)
    scale = (MLA_NOPE + MLA_ROPE) ** -0.5
    chunk_id = jnp.arange(S) // CHUNK
    outs = []
    for i in range(S // Q_BLOCK):
        q0, q1 = i * Q_BLOCK, (i + 1) * Q_BLOCK
        s = (jnp.einsum('bqhd,bkhd->bhqk', q_nope[:, q0:q1], k_nope[:, :q1])
             + jnp.einsum('bqhr,bkr->bhqk', q_pe[:, q0:q1], k_pe[:, :q1])).astype(jnp.float32) * scale
        mask = chunk_id[None, :q1] <= chunk_id[q0:q1, None]
        p = jax.nn.softmax(jnp.where(mask, s, -jnp.inf), axis=-1).astype(v.dtype)
        outs.append(jnp.einsum('bhqk,bkhd->bqhd', p, v[:, :q1]))
    o = jnp.concatenate(outs, axis=1)
    return o.reshape(B, S, MLA_HEADS * MLA_V)

def gated_delta_chunked(q, k, v, g, beta):
    B, S, H, DK = q.shape
    DV = v.shape[-1]
    N = S // CHUNK

    def to_chunks(t):
        return jnp.moveaxis(t.reshape((B, N, CHUNK, H) + t.shape[3:]), 3, 1)

    q = to_chunks(q) * (DK ** -0.5)
    k = to_chunks(k)
    v = to_chunks(v)
    beta = to_chunks(beta)
    g = jnp.cumsum(to_chunks(g), axis=-1)
    idx = jnp.arange(CHUNK)
    incl = idx[:, None] >= idx[None, :]
    strict = idx[:, None] > idx[None, :]
    decay = jnp.exp(jnp.where(incl, g[..., :, None] - g[..., None, :], -jnp.inf))
    kb = k * beta[..., None]
    vb = v * beta[..., None]
    L = jnp.where(strict, jnp.einsum('bhncd,bhnmd->bhncm', kb, k) * decay, 0.0)
    eye = jnp.eye(CHUNK, dtype=jnp.float32)
    T = lax.linalg.triangular_solve(eye + L, jnp.broadcast_to(eye, L.shape), left_side=True,
                                    lower=True, unit_diagonal=True)
    u = T @ vb
    w = T @ (kb * jnp.exp(g)[..., None])
    A = jnp.einsum('bhncd,bhnmd->bhncm', q, k) * decay
    qg = q * jnp.exp(g)[..., None]
    kd = k * jnp.exp(g[..., -1:] - g)[..., None]
    g_last = jnp.exp(g[..., -1])

    def step(state, xs):
        qg_c, kd_c, u_c, w_c, A_c, gl = xs
        v_new = u_c - jnp.einsum('bhcd,bhde->bhce', w_c, state)
        o = jnp.einsum('bhcd,bhde->bhce', qg_c, state) + jnp.einsum('bhcm,bhme->bhce', A_c, v_new)
        state = state * gl[..., None, None] + jnp.einsum('bhcd,bhce->bhde', kd_c, v_new)
        return state, o

    xs = tuple(jnp.moveaxis(t, 2, 0) for t in (qg, kd, u, w, A, g_last))
    state0 = jnp.zeros((B, H, DK, DV), jnp.float32)
    _, o = lax.scan(step, state0, xs)
    o = jnp.moveaxis(o, 0, 2)
    return jnp.moveaxis(o, 1, 3).reshape(B, S, H, DV)

def gdn_group(qkv, z, a, b, conv_w, a_log, dt_bias, norm_w):
    B, S, _ = qkv.shape
    qkv = jax.nn.silu(causal_depthwise_conv(qkv, conv_w)).astype(jnp.float32)
    q, k, v = jnp.split(qkv, [GDN_HEADS * GDN_DK, 2 * GDN_HEADS * GDN_DK], axis=-1)
    q = l2norm(q.reshape(B, S, GDN_HEADS, GDN_DK))
    k = l2norm(k.reshape(B, S, GDN_HEADS, GDN_DK))
    v = v.reshape(B, S, GDN_HEADS, GDN_DV)
    beta = jax.nn.sigmoid(b.astype(jnp.float32))
    g = -jnp.exp(a_log.astype(jnp.float32)) * jax.nn.softplus(a.astype(jnp.float32) + dt_bias.astype(jnp.float32))
    o = gated_delta_chunked(q, k, v, g, beta)
    o = rms_norm(o, norm_w) * jax.nn.silu(z.astype(jnp.float32).reshape(B, S, GDN_HEADS, GDN_DV))
    return o.reshape(B, S, GDN_HEADS * GDN_DV).astype(z.dtype)

def moe(h, router_w, router_bias, w_gate, w_up, w_down, sh_gate, sh_up, sh_down):
    B, S, D = h.shape
    xt = h.reshape(-1, D)
    N = xt.shape[0]
    scores = jax.nn.sigmoid((xt @ router_w).astype(jnp.float32))
    biased = scores + router_bias.astype(jnp.float32)
    grp = biased.reshape(N, N_GROUPS, N_EXPERTS // N_GROUPS)
    grp_score = lax.top_k(grp, 2)[0].sum(-1)
    _, top_g = lax.top_k(grp_score, TOPK_GROUPS)
    gmask = jnp.any(top_g[:, :, None] == jnp.arange(N_GROUPS)[None, None, :], axis=1)
    emask = jnp.repeat(gmask, N_EXPERTS // N_GROUPS, axis=1)
    _, top_e = lax.top_k(jnp.where(emask, biased, -jnp.inf), TOP_K)
    wts = jnp.take_along_axis(scores, top_e, axis=1)
    wts = wts / jnp.sum(wts, axis=-1, keepdims=True) * ROUTED_SCALE
    NK = N * TOP_K
    flat_e = top_e.reshape(-1).astype(jnp.int32)
    flat_tok = jnp.arange(NK, dtype=jnp.int32) // TOP_K
    flat_w = wts.reshape(-1)
    order = jnp.argsort(flat_e, stable=True)
    sorted_e = flat_e[order]
    counts = jnp.bincount(flat_e, length=N_EXPERTS).astype(jnp.int32)
    padded = (counts + MOE_BLOCK - 1) // MOE_BLOCK * MOE_BLOCK
    pad_end = jnp.cumsum(padded)
    pad_start = pad_end - padded
    start = jnp.cumsum(counts) - counts
    dest = pad_start[sorted_e] + jnp.arange(NK, dtype=jnp.int32) - start[sorted_e]
    n_blocks = -(-NK // MOE_BLOCK) + N_EXPERTS
    P = n_blocks * MOE_BLOCK
    buf_tok = jnp.zeros((P,), jnp.int32).at[dest].set(flat_tok[order])
    buf_w = jnp.zeros((P,), jnp.float32).at[dest].set(flat_w[order])
    block_e = jnp.clip(jnp.searchsorted(pad_end, jnp.arange(n_blocks, dtype=jnp.int32) * MOE_BLOCK, side='right'),
                       0, N_EXPERTS - 1).astype(jnp.int32)

    def body(acc, blk):
        tok, wt, e = blk
        xb = xt[tok]
        hb = jax.nn.silu(xb @ w_gate[e]) * (xb @ w_up[e])
        yb = (hb @ w_down[e]).astype(jnp.float32)
        return acc.at[tok].add(yb * wt[:, None]), None

    acc, _ = lax.scan(body, jnp.zeros((N, D), jnp.float32),
                      (buf_tok.reshape(n_blocks, MOE_BLOCK), buf_w.reshape(n_blocks, MOE_BLOCK), block_e))
    shared = (jax.nn.silu(xt @ sh_gate) * (xt @ sh_up)) @ sh_down
    return (acc + shared.astype(jnp.float32)).astype(h.dtype).reshape(B, S, D)

def setup_inputs(seed: int = 0) -> dict:
    key = jax.random.key(seed)
    ks = jax.random.split(key, 27)
    f32 = jnp.float32
    L, D = DEPTH, D_MODEL

    def nrm(k, shape, fan_in):
        return jax.random.normal(k, shape, f32) * (fan_in ** -0.5)

    def gain(k, shape):
        return 1.0 + 0.02 * jax.random.normal(k, shape, f32)

    x = jax.random.normal(ks[0], (BATCH, SEQ, D), f32)
    c = jax.random.normal(ks[1], (BATCH, D), f32)
    offset = jax.random.randint(ks[2], (BATCH, 1), 0, 64, dtype=jnp.int32) * CHUNK
    positions = offset + jnp.arange(SEQ, dtype=jnp.int32)[None, :]
    ada_w = nrm(ks[3], (L, D, 6 * D), D) * 0.5
    ada_b = 0.02 * jax.random.normal(ks[4], (L, 6 * D), f32)
    norm1_w = gain(ks[5], (L, D))
    w_in = nrm(ks[6], (L, D, D_IN), D)
    q_a_norm_w = gain(ks[7], (L, MLA_Q_RANK))
    wq_b = nrm(ks[8], (L, MLA_Q_RANK, MLA_HEADS * (MLA_NOPE + MLA_ROPE)), MLA_Q_RANK)
    kv_a_norm_w = gain(ks[9], (L, MLA_KV_RANK))
    wkv_b = nrm(ks[10], (L, MLA_KV_RANK, MLA_HEADS * (MLA_NOPE + MLA_V)), MLA_KV_RANK)
    gdn_conv_w = nrm(ks[11], (L, GDN_CONV, GDN_QKV), GDN_CONV)
    gdn_a_log = jnp.log(jax.random.uniform(ks[12], (L, GDN_HEADS), f32, 1.0, 16.0))
    dt = jnp.exp(jax.random.uniform(ks[13], (L, GDN_HEADS), f32, math.log(1e-3), math.log(1e-1)))
    gdn_dt_bias = dt + jnp.log(-jnp.expm1(-dt))
    gdn_norm_w = gain(ks[14], (L, GDN_DV))
    w_out = nrm(ks[15], (L, MIX_WIDTH, D), MIX_WIDTH)
    norm2_w = gain(ks[16], (L, D))
    router_w = nrm(ks[17], (L, D, N_EXPERTS), D)
    router_bias = 0.01 * jax.random.normal(ks[18], (L, N_EXPERTS), f32)
    exp_w_gate = nrm(ks[19], (L, N_EXPERTS, D, D_EXPERT), D)
    exp_w_up = nrm(ks[20], (L, N_EXPERTS, D, D_EXPERT), D)
    exp_w_down = nrm(ks[21], (L, N_EXPERTS, D_EXPERT, D), D_EXPERT)
    sh_w_gate = nrm(ks[22], (L, D, D_SHARED), D)
    sh_w_up = nrm(ks[23], (L, D, D_SHARED), D)
    sh_w_down = nrm(ks[24], (L, D_SHARED, D), D_SHARED)
    final_norm_w = gain(ks[25], (D,))
    return {'x': x, 'c': c, 'positions': positions, 'ada_w': ada_w, 'ada_b': ada_b, 'norm1_w': norm1_w,
            'w_in': w_in, 'q_a_norm_w': q_a_norm_w, 'wq_b': wq_b, 'kv_a_norm_w': kv_a_norm_w, 'wkv_b': wkv_b,
            'gdn_conv_w': gdn_conv_w, 'gdn_a_log': gdn_a_log, 'gdn_dt_bias': gdn_dt_bias, 'gdn_norm_w': gdn_norm_w,
            'w_out': w_out, 'norm2_w': norm2_w, 'router_w': router_w, 'router_bias': router_bias,
            'exp_w_gate': exp_w_gate, 'exp_w_up': exp_w_up, 'exp_w_down': exp_w_down,
            'sh_w_gate': sh_w_gate, 'sh_w_up': sh_w_up, 'sh_w_down': sh_w_down, 'final_norm_w': final_norm_w}

def reference(x, c, positions, ada_w, ada_b, norm1_w, w_in, q_a_norm_w, wq_b, kv_a_norm_w, wkv_b,
              gdn_conv_w, gdn_a_log, gdn_dt_bias, gdn_norm_w, w_out, norm2_w, router_w, router_bias,
              exp_w_gate, exp_w_up, exp_w_down, sh_w_gate, sh_w_up, sh_w_down, final_norm_w):
    split_at = np.cumsum(IN_SPLITS)[:-1].tolist()
    for l in range(DEPTH):
        mod = jax.nn.silu(c) @ ada_w[l] + ada_b[l]
        sh1, sc1, g1, sh2, sc2, g2 = [m[:, None, :] for m in jnp.split(mod, 6, axis=-1)]
        h = rms_norm(x, norm1_w[l]) * (1.0 + sc1) + sh1
        proj = h @ w_in[l]
        c_q, c_kv, k_pe, qkv, z, a, b = jnp.split(proj, split_at, axis=-1)
        out_a = mla_group(c_q, c_kv, k_pe, positions, q_a_norm_w[l], wq_b[l], kv_a_norm_w[l], wkv_b[l])
        out_b = gdn_group(qkv, z, a, b, gdn_conv_w[l], gdn_a_log[l], gdn_dt_bias[l], gdn_norm_w[l])
        mix = jnp.concatenate([out_a, out_b], axis=-1) @ w_out[l]
        x = x + g1 * mix
        h2 = rms_norm(x, norm2_w[l]) * (1.0 + sc2) + sh2
        x = x + g2 * moe(h2, router_w[l], router_bias[l], exp_w_gate[l], exp_w_up[l], exp_w_down[l],
                         sh_w_gate[l], sh_w_up[l], sh_w_down[l])
    return rms_norm(x, final_norm_w)


_drawn_inputs = setup_inputs


def setup_inputs(seed=0):
    import zlib

    import numpy as np

    out = dict(_drawn_inputs(seed))
    spreads = {}
    factors = {'norm1_w': 3.878,
     'q_a_norm_w': 8.0,
     'kv_a_norm_w': 8.0,
     'gdn_norm_w': 14.793,
     'final_norm_w': 7.758,
     'norm2_w': 5.964,
     'router_bias': 4.01}
    for name, (base, spread) in spreads.items():
        noise = np.random.default_rng([zlib.crc32(name.encode()), seed]).standard_normal(out[name].shape)
        drawn = base * np.exp(spread * noise) if base else spread * noise
        out[name] = jnp.asarray(drawn.astype(out[name].dtype))
    for name, factor in factors.items():
        out[name] = (out[name] * factor).astype(out[name].dtype)
    return out
```

```python
from contextlib import ExitStack

import numpy as np

import concourse.bass as bass
from concourse import mybir

F32 = mybir.dt.float32
I32 = mybir.dt.int32
U32 = mybir.dt.uint32
ALU = mybir.AluOpType
ACT = mybir.ActivationFunctionType
AX = mybir.AxisListType

P = 128
S = 1024
D = 1024
NT = S // P
KD = D // P
HALF = 512
H = 4
QR, KVR, ROPE, NOPE = 384, 256, 64, 128
KQ, KV = QR // P, KVR // P
QH = NOPE + ROPE
CHUNK = 64
EPS = 1e-6
MLA_SCALE = float(QH) ** -0.5
THETA = 10000.0
COL_CQ, COL_CKV, COL_KPE, COL_QKV = 0, QR, QR + KVR, QR + KVR + ROPE
COL_Z = COL_QKV + 3 * H * P
COL_AB = COL_Z + H * P
D_IN = COL_AB + 2 * H
LEVELS = 6
TWO_PI = 2 * np.pi
ROUND = 1.5 * 2.0 ** 23
NEG = -1e30

V_C, V_N1, V_N2, V_QA, V_KVA = 0, 8, 16, 24, 27
V_CONV = 29
V_ADAB = 77
V_GN = 125
NVEC = 126

C_ID, C_UP, C_ONEB, C_MASK = 0, P, 2 * P, 3 * P
C_INVF = C_MASK + LEVELS * P
C_SIGN = C_INVF + 1
C_STRICT = C_INVF + 2
C_COLS = C_STRICT + P


def shape_constants():
    c = np.zeros((P, C_COLS), np.float32)
    m, n = np.arange(P)[:, None], np.arange(P)[None, :]
    same = m // CHUNK == n // CHUNK
    c[:, C_ID:C_ID + P] = m == n
    c[:, C_UP:C_UP + P] = (m <= n) & same
    c[:, C_ONEB:C_ONEB + P] = same
    for level in range(LEVELS):
        b = 2 ** level
        c[:, C_MASK + level * P:C_MASK + (level + 1) * P] = (m // (2 * b) == n // (2 * b)) & (n % (2 * b) >= b) & (m % (2 * b) < b)
    inv = 1.0 / (np.float32(THETA) ** (np.arange(0, ROPE, 2, dtype=np.float32) / np.float32(ROPE)))
    c[:, C_INVF] = np.tile(inv.astype(np.float32), P // (ROPE // 2))
    c[:, C_SIGN] = np.where(np.arange(P) % ROPE < ROPE // 2, -1.0, 1.0)
    c[:, C_STRICT:C_STRICT + P] = m < n
    return c


def late_constants():
    return np.concatenate([np.tile(np.arange(P, dtype=np.float32), (P, 1)),
                           (np.arange(P)[:, None] + P * np.arange(NT)[None, :]).astype(np.float32)], axis=1)

def hybrid_block(nc, A, out):
    ctx = ExitStack()
    with ctx:
        def sb(name, cols, dt=F32):
            return ctx.enter_context(nc.sbuf_tensor(name, [P, cols], dt))

        def sem(name):
            return ctx.enter_context(nc.semaphore(name))

        r_h = sb("r_h", 8 * S)
        r_ring = sb("r_ring", 3 * 4096)
        r_qkv = sb("r_qkv", 12 * S)
        r_z = sb("r_z", 4 * S)
        r_work = sb("r_work", 13 * S)
        consts = sb("consts", C_COLS)
        ones = sb("ones", P)
        vecrows = sb("vecrows", P)
        vec = sb("vec", NVEC)
        bias = sb("bias", 4)
        csil = sb("csil", KD)
        modc = sb("modc", 48)
        gain1 = sb("gain1", KD)
        gain2 = sb("gain2", KD)
        ssq = sb("ssq", KD)
        std = sb("std", KD)
        rstd = sb("rstd", KD)
        wab = sb("wab", KD * 8)
        ab = sb("ab", NT * 8)
        heads = sb("heads", 2 * H)
        negrate = sb("negrate", 2 * H)
        ncol = sb("ncol", 10 * NT)
        rcol = sb("rcol", 10 * NT)
        g = sb("g", NT * H)
        gtmp = sb("gtmp", 3 * NT * H)
        beta = sb("beta", NT * H)
        gcs = sb("gcs", NT * H)
        egc = sb("egc", NT * H)
        ekd = sb("ekd", NT * H)
        egl = sb("egl", 2 * NT * H)
        rowmax = sb("rowmax", NT * H)
        negmax = sb("negmax", NT * H)
        rowsum = sb("rowsum", NT * H)
        rowinv = sb("rowinv", NT * H)
        pair = [ctx.enter_context(nc.psum_tensor(f"pair{i}", [P, 2 * HALF], F32)) for i in range(4)]

        def bank(i):
            return pair[i // 2][:, (i % 2) * HALF:(i % 2) * HALF + HALF]

        ident = consts[:, C_ID:C_ID + P]
        upper = consts[:, C_UP:C_UP + P]
        hT = r_h[:, :].rearrange("p (k n) -> p k n", k=KD)
        ring = [r_ring[:, 4096 * i:4096 * (i + 1)] for i in range(3)]
        x_in = r_qkv[:, 0:NT * D].rearrange("p (t n) -> p t n", t=NT)
        qkvT = r_qkv[:, :].rearrange("p (j n) -> p j n", j=12)
        zT = r_z[:, :].rearrange("p (j n) -> p j n", j=H)
        work = r_work[:, :].rearrange("p (j n) -> p j n", j=13)
        cqT, ckvT, kpe, kpe_sw = work[:, 0:3], work[:, 3:5], work[:, 5], work[:, 6]
        cosT, sinT = work[:, 7], work[:, 8]
        sq, diag = work[:, 9:11], work[:, 11:13]
        conv = sq
        wkpe = r_work[:, 11 * S:13 * S].rearrange("p (k n) -> p k n", k=KD)
        ang = [qkvT[:, 8 + i] for i in range(4)]
        pos = ang[0].bitcast(I32)

        def rows(name):
            return A[name].rearrange("(r p) -> r p", p=P)

        vec_loads = [(V_C, 8, A["c"].rearrange("a (r p) -> (a r) p", p=P)),
                     (V_N1, 8, A["norm1_w"].rearrange("a (r p) -> (a r) p", p=P)),
                     (V_N2, 8, A["norm2_w"].rearrange("a (r p) -> (a r) p", p=P)),
                     (V_QA, 3, A["q_a_norm_w"].rearrange("a (r p) -> (a r) p", p=P)),
                     (V_KVA, 2, A["kv_a_norm_w"].rearrange("a (r p) -> (a r) p", p=P)),
                     (V_CONV, 48, A["gdn_conv_w"].rearrange("a t (r p) -> (a t r) p", p=P)),
                     (V_ADAB, 48, A["ada_b"].rearrange("a (r p) -> (a r) p", p=P)),
                     (V_GN, 1, A["gdn_norm_w"])]
        setup_loads = [(consts[:, :], A["shape_constants"]),
                       (pos, A["positions"][0].partition_broadcast(P)),
                       (heads[:, 0:H], A["gdn_a_log"][0].partition_broadcast(P)),
                       (heads[:, H:2 * H], A["gdn_dt_bias"][0].partition_broadcast(P)),
                       (wab[:, :].rearrange("p (k n) -> p k n", k=KD),
                        A["w_in"][0].rearrange("(k p) n -> p k n", p=P)[:, :, COL_AB:D_IN])]
        setup_loads += [(vecrows[r:r + n, :], src) for r, n, src in vec_loads]
        N_SETUP = 16 * len(setup_loads)

        w_in = A["w_in"][0].rearrange("(k p) n -> p k n", p=P)
        ada = A["ada_w"][0].rearrange("(k p) n -> p k n", p=P)
        wq = A["wq_b"][0].rearrange("(k p) n -> p k n", p=P)
        wkv = A["wkv_b"][0].rearrange("(k p) n -> p k n", p=P)

        def cols(w, a, b):
            return w[:, :, a:b]

        ring_loads = [cols(ada, j * HALF, (j + 1) * HALF) for j in range(4)]
        ring_loads += [cols(w_in, COL_QKV + j * HALF, COL_QKV + (j + 1) * HALF) for j in range(3)]
        ring_loads += [cols(w_in, COL_Z, COL_AB), cols(w_in, 0, COL_CKV), cols(w_in, COL_CKV, COL_QKV), wq, wkv]
        L_QKV, L_Z, L_CQ, L_CKV, L_WQ, L_WKV = 4, 7, 8, 9, 10, 11

        def slot(n):
            k, w = ring_loads[n].shape[1:]
            return ring[n % 3][:, 0:k * w].rearrange("p (k n) -> p k n", k=k)

        wqpe = ring[L_WQ % 3][:, KQ * H * QH:KQ * H * QH + KQ * 4 * P].rearrange("p (k n) -> p k n", k=KQ)
        qT = r_h[:, 0:4 * S].rearrange("p (h n) -> p h n", h=H)
        kT = r_h[:, 4 * S:8 * S].rearrange("p (h n) -> p h n", h=H)
        v_tok = ring[0].rearrange("p (t n) -> p t n", t=NT)
        oT_mla = ring[1].rearrange("p (h n) -> p h n", h=H)
        prob = ring[2][:, 0:2 * S].rearrange("p (b n) -> p b n", b=2)
        probT = ring[2][:, 2 * S:4 * S].rearrange("p (b n) -> p b n", b=2)
        qpe, qpe_sw = work[:, 11:13], work[:, 9:11]
        oT_gdn = qkvT[:, 8:12]

        groups = []

        def by_features(w, k_tiles, src, dst, load, func=ACT.Copy):
            for half in range(2):
                at = slice(half * HALF, (half + 1) * HALF)
                groups.append(([(w(k), src[:, k, at]) for k in range(k_tiles)], dst[:, at], func, load))

        def block_cols(n, a, width=P):
            return lambda k: slot(n)[:, k, a:a + width]

        for j in range(12):
            by_features(block_cols(L_QKV + j // 4, (j % 4) * P), KD, hT, qkvT[:, j], L_QKV + j // 4)
        for j in range(H):
            by_features(block_cols(L_Z, j * P), KD, hT, zT[:, j], L_Z, ACT.Silu)
        for j in range(KQ):
            by_features(block_cols(L_CQ, j * P), KD, hT, cqT[:, j], L_CQ)
        for j in range(KV):
            by_features(block_cols(L_CKV, j * P), KD, hT, ckvT[:, j], L_CKV)
        by_features(lambda k: wkpe[:, k, 0:P], KD, hT, kpe, None)
        by_features(lambda k: wkpe[:, k, P:2 * P], KD, hT, kpe_sw, None)
        G_KPE = len(groups) - 4
        G_AB = len(groups)
        groups.append((None, ab[:, :], ACT.Copy, None))
        G_LAT = len(groups)
        for h in range(H):
            by_features(block_cols(L_WQ, h * QH), KQ, cqT, qT[:, h], L_WQ)
        for i in range(2):
            by_features(lambda k, i=i: wqpe[:, k, i * P:(i + 1) * P], KQ, cqT, qpe[:, i], None)
            by_features(lambda k, i=i: wqpe[:, k, (2 + i) * P:(3 + i) * P], KQ, cqT, qpe_sw[:, i], None)
        G_KV = len(groups)
        for h in range(H):
            by_features(block_cols(L_WKV, h * (NOPE + P)), KV, ckvT, kT[:, h], L_WKV)
        v_cols = slot(L_WKV).rearrange("p k (h n) -> p k h n", h=H)[:, :, :, NOPE:NOPE + P]
        for t in range(NT):
            groups.append(([(ckvT[:, k, t * P:(t + 1) * P], v_cols[:, k]) for k in range(KV)],
                           v_tok[:, t], ACT.Copy, L_WKV))
        N_GROUPS = len(groups)

        def last_group(load):
            return max(i for i, gr in enumerate(groups) if gr[3] == load)

        norm_jobs = [([cqT[:, k] for k in range(KQ)], V_QA), ([ckvT[:, k] for k in range(KV)], V_KVA)]
        norm_jobs += [([qkvT[:, j]], None) for j in range(8)]
        N_JOBS = len(norm_jobs)
        norm_tiles = [(n, k, len(srcs), src) for n, (srcs, _) in enumerate(norm_jobs) for k, src in enumerate(srcs)]

        setup_loaded = sem("setup_loaded")
        x_loaded = [sem(f"x_loaded{t}") for t in range(NT)]
        ring_loaded = [sem(f"ring_loaded{i}") for i in range(3)]
        bias_set = sem("bias_set")
        vecT_ready = sem("vecT_ready")
        vec_ready = sem("vec_ready")
        csil_ready = sem("csil_ready")
        mod_ready = sem("mod_ready")
        angles_ready = sem("angles_ready")
        tables_ready = sem("tables_ready")
        ssq_ready = sem("ssq_ready")
        std_ready = sem("std_ready")
        xn_ready = sem("xn_ready")
        xT_ready = sem("xT_ready")
        gain1_ready = sem("gain1_ready")
        hT_act = sem("hT_act")
        hT_dve = sem("hT_dve")
        proj_ready = sem("proj_ready")
        proj_stored = sem("proj_stored")
        conv_ready = sem("conv_ready")
        conv_stored = sem("conv_stored")
        wpe_ready = sem("wpe_ready")
        squares_ready = sem("squares_ready")
        sumsq_ready = sem("sumsq_ready")
        ncol_ready = sem("ncol_ready")
        diag_ready = sem("diag_ready")
        spread_ready = sem("spread_ready")
        normed = sem("normed")
        roped = sem("roped")
        ab_parts = sem("ab_parts")
        g_ready = sem("g_ready")
        gcum_ready = sem("gcum_ready")
        gexp_ready = sem("gexp_ready")
        ekd_in = sem("ekd_in")
        scores_ready = sem("scores_ready")
        negmax_ready = sem("negmax_ready")
        exp_ready = sem("exp_ready")
        prob_ready = sem("prob_ready")
        probT_ready = sem("probT_ready")
        probT_stored = sem("probT_stored")
        pv_ready = sem("pv_ready")
        o_stored = sem("o_stored")
        vector_step = sem("vector_step")
        score_tiles = [(i, h) for i in range(NT) for h in range(H)]
        N_ST = len(score_tiles)

        NG = NT * H
        HP = H * P

        def buffers(first):
            return [r_work[:, (first * 2 + s) * HP:(first * 2 + s + 1) * HP].rearrange("p (h n) -> p h n", h=H) for s in range(2)]

        (ug, dm, egrow, at_, lt, lo, tri, triT, m1, kg, kd, vt, qg) = (buffers(i) for i in range(13))
        nw = lo
        vnew = [ring[2][:, (2 + c) * HP:(3 + c) * HP].rearrange("p (h n) -> p h n", h=H) for c in range(2)]
        state = [ring[2][:, c * HP:(c + 1) * HP].rearrange("p (h n) -> p h n", h=H) for c in range(2)]

        def over_heads(m):
            return m.unsqueeze(1).broadcast_to([P, H, P])

        def per_head(scalars, t):
            return scalars[:, t * H:(t + 1) * H].unsqueeze(2).broadcast_to([P, H, P])

        def hb(i):
            return bank(i).rearrange("p (h n) -> p h n", h=H)

        def mask(level):
            return over_heads(consts[:, C_MASK + level * P:C_MASK + (level + 1) * P])

        zeroed = sem("zeroed")
        ug_ready = sem("ug_ready")
        grow_ready = sem("grow_ready")
        kk_ready = sem("kk_ready")
        qk_ready = sem("qk_ready")
        ktok_ready = sem("ktok_ready")
        vtok_ready = sem("vtok_ready")
        expo_ready = sem("expo_ready")
        egrow_ready = sem("egrow_ready")
        decay_ready = sem("decay_ready")
        at_ready = sem("at_ready")
        lt_ready = sem("lt_ready")
        kg_ready = sem("kg_ready")
        kd_ready = sem("kd_ready")
        vt_ready = sem("vt_ready")
        qg_ready = sem("qg_ready")
        lo_ready = [sem(f"lo_ready{s}") for s in range(2)]
        m_ready = [sem(f"m_ready{s}") for s in range(2)]
        m1_ready = [sem(f"m1_ready{s}") for s in range(2)]
        p_ready = [sem(f"p_ready{s}") for s in range(2)]
        tri_ready = [sem(f"tri_ready{s}") for s in range(2)]
        w_ready = sem("w_ready")
        nw_ready = sem("nw_ready")
        vn_ready = sem("vn_ready")
        vnew_ready = sem("vnew_ready")
        sup_ready = sem("sup_ready")
        state_ready = sem("state_ready")
        og_ready = sem("og_ready")
        og_stored = sem("og_stored")

        def tile_cols(t):
            return slice(t * P, (t + 1) * P)

        def gdn_pool(pool):
            tt = nc.gpsimd.tensor_tensor
            pool.wait_ge(o_stored, N_ST)
            for c in range(2):
                nc.gpsimd.memset(state[c], 0.0)
                nc.gpsimd.memset(vnew[c], 0.0).then_inc(zeroed, 1)
            for tp in range(NT // 2):
                for s in range(2):
                    t = 2 * tp + s
                    if t >= 2:
                        pool.wait_ge(grow_ready, t - 1)
                    tt(ug[s], over_heads(upper), per_head(g, t), ALU.mult).then_inc(ug_ready, 1)
                for s in range(2):
                    t = 2 * tp + s
                    pool.wait_ge(egrow_ready, t + 1)
                    if t >= 2:
                        pool.wait_ge(og_ready, 2 * t - 2)
                    tt(qg[s], qkvT[:, 0:H, tile_cols(t)], egrow[s], ALU.mult).then_inc(qg_ready, 1)
                for level in range(LEVELS):
                    for s in range(2):
                        t = 2 * tp + s
                        if level == 0:
                            pool.wait_ge(lt_ready, t + 1)
                            if t >= 2:
                                pool.wait_ge(vn_ready, 2 * t - 2)
                        elif level == 1:
                            pool.wait_ge(tri_ready[s], LEVELS * tp + 1)
                        else:
                            pool.wait_ge(m_ready[s], LEVELS * tp + level)
                        tt(lo[s], lt[s], mask(level), ALU.mult).then_inc(lo_ready[s], 1)

        def gdn_pe(pe):
            mm = nc.tensor.matmul
            for tp in range(NT // 2):
                for s in range(2):
                    t = 2 * tp + s
                    X = 3 * s
                    if t >= 2:
                        pe.wait_ge(og_stored, 2 * t - 2)
                        pe.wait_ge(state_ready, 2 * t - 2)
                    pe.wait_ge(ug_ready, t + 1)
                    mm(bank(X), ones[:, :], ug[s], start=True, stop=True).then_inc(grow_ready, 1)
                    for h in range(H):
                        kt = qkvT[:, H + h, tile_cols(t)]
                        last = mm(hb(X + 1)[:, h], kt, kt, start=True, stop=True)
                    last.then_inc(kk_ready, 1)
                    for h in range(H):
                        last = mm(hb(X + 2)[:, h], qkvT[:, H + h, tile_cols(t)], qkvT[:, h, tile_cols(t)], start=True, stop=True)
                    last.then_inc(qk_ready, 1)
                    if t >= 1:
                        pe.wait_ge(kg_ready, t)
                        pe.wait_ge(kd_ready, t)
                        pe.wait_ge(vt_ready, t)
                    for h in range(H):
                        last = nc.tensor.transpose(hb(6)[:, h], qkvT[:, H + h, tile_cols(t)], ident)
                    last.then_inc(ktok_ready, 1)
                    for h in range(H):
                        last = nc.tensor.transpose(hb(7)[:, h], qkvT[:, 2 * H + h, tile_cols(t)], ident)
                    last.then_inc(vtok_ready, 1)
                for level in range(LEVELS):
                    for s in range(2):
                        t = 2 * tp + s
                        X = 3 * s
                        pe.wait_ge(lo_ready[s], LEVELS * tp + level + 1)
                        if level == 0:
                            pe.wait_ge(decay_ready, t + 1)
                            pe.wait_ge(expo_ready, t + 1)
                            pe.wait_ge(egrow_ready, t + 1)
                        else:
                            pe.wait_ge(tri_ready[s], LEVELS * tp + level)
                        for h in range(H):
                            last = mm(hb(X)[:, h], lo[s][:, h], ident if level == 0 else tri[s][:, h], start=True, stop=True)
                        last.then_inc(m_ready[s], 1)
                    if level == 0:
                        continue
                    for s in range(2):
                        X = 3 * s
                        pe.wait_ge(m1_ready[s], (LEVELS - 1) * tp + level)
                        for h in range(H):
                            last = mm(hb(X + 2)[:, h], m1[s][:, h], triT[s][:, h], start=True, stop=True)
                        if level < LEVELS - 1:
                            for h in range(H):
                                last = mm(hb(X + 1)[:, h], triT[s][:, h], m1[s][:, h], start=True, stop=True)
                        last.then_inc(p_ready[s], 1)
                for s in range(2):
                    t = 2 * tp + s
                    pe.wait_ge(tri_ready[s], LEVELS * (tp + 1))
                    pe.wait_ge(kg_ready, t + 1)
                    for h in range(H):
                        last = mm(hb(3 * s)[:, h], kg[s][:, h], triT[s][:, h], start=True, stop=True)
                    last.then_inc(w_ready, 1)
                for s in range(2):
                    t = 2 * tp + s
                    X = 3 * s
                    pe.wait_ge(nw_ready, t + 1)
                    pe.wait_ge(vt_ready, t + 1)
                    pe.wait_ge(kd_ready, t + 1)
                    pe.wait_ge(qg_ready, t + 1)
                    if t == 0:
                        pe.wait_ge(zeroed, 2)
                    for c in range(2):
                        n = 2 * t + c
                        if n >= 1:
                            pe.wait_ge(state_ready, n)
                            pe.wait_ge(vnew_ready, n)
                        for h in range(H):
                            mm(hb(X + 1)[:, h], triT[s][:, h], vt[s][:, h], start=True, stop=False)
                            last = mm(hb(X + 1)[:, h], nw[s][:, h], state[n % 2][:, h], start=False, stop=True)
                        last.then_inc(vn_ready, 1)
                        pe.wait_ge(vnew_ready, n + 1)
                        for h in range(H):
                            last = mm(hb(X)[:, h], kd[s][:, h], vnew[c][:, h], start=True, stop=True)
                        last.then_inc(sup_ready, 1)
                        pe.wait_ge(at_ready, t + 1)
                        if c == 1:
                            pe.wait_ge(og_stored, n)
                        at = slice(c * CHUNK, (c + 1) * CHUNK)
                        for h in range(H):
                            mm(hb(X + 2)[:, h, at], state[n % 2][:, h], qg[s][:, h, at], start=True, stop=False)
                            last = mm(hb(X + 2)[:, h, at], vnew[c][:, h], at_[s][:, h, at], start=False, stop=True)
                        last.then_inc(og_ready, 1)

        def gdn_act(act):
            do = nc.scalar.activation
            for tp in range(NT // 2):
                for s in range(2):
                    t = 2 * tp + s
                    act.wait_ge(expo_ready, t + 1)
                    if t >= 2:
                        act.wait_ge(qg_ready, t - 1)
                    do(egrow[s], hb(3 * s), ACT.Exp).then_inc(egrow_ready, 1)
                    do(dm[s], dm[s], ACT.Exp).then_inc(decay_ready, 1)
                    act.wait_ge(vtok_ready, t + 1)
                    do(vt[s], hb(7), ACT.Copy).then_inc(vt_ready, 1)
                for level in range(1, LEVELS):
                    for s in range(2):
                        act.wait_ge(m_ready[s], LEVELS * tp + level + 1)
                        if level >= 2:
                            act.wait_ge(p_ready[s], (LEVELS - 1) * tp + level - 1)
                        do(m1[s], hb(3 * s), ACT.Copy).then_inc(m1_ready[s], 1)
                for s in range(2):
                    t = 2 * tp + s
                    act.wait_ge(w_ready, t + 1)
                    do(nw[s], hb(3 * s), ACT.Copy, scale=-1.0).then_inc(nw_ready, 1)
                for s in range(2):
                    t = 2 * tp + s
                    for c in range(2):
                        n = 2 * t + c
                        act.wait_ge(og_ready, n + 1)
                        at = slice(c * CHUNK, (c + 1) * CHUNK)
                        do(oT_gdn[:, :, t * P + c * CHUNK:t * P + (c + 1) * CHUNK], hb(3 * s + 2)[:, :, at], ACT.Copy)\
                            .then_inc(og_stored, 1)

        def gdn_dve(dve, then):
            v = nc.vector
            for tp in range(NT // 2):
                for s in range(2):
                    t = 2 * tp + s
                    X = 3 * s
                    dve.wait_ge(grow_ready, t + 1)
                    dve.wait_ge(gexp_ready, 3)
                    then(v.tensor_tensor(dm[s], hb(X), per_head(gcs, t), ALU.subtract))
                    v.tensor_scalar(dm[s], dm[s], 0.0, None, ALU.min).then_inc(expo_ready, 1)
                for s in range(2):
                    t = 2 * tp + s
                    X = 3 * s
                    dve.wait_ge(ktok_ready, t + 1)
                    v.tensor_tensor(kg[s], hb(6), per_head(egc, t), ALU.mult).then_inc(kg_ready, 1)
                    v.tensor_tensor(kd[s], hb(6), per_head(ekd, t), ALU.mult).then_inc(kd_ready, 1)
                    dve.wait_ge(decay_ready, t + 1)
                    then(v.tensor_tensor(dm[s], dm[s], over_heads(upper), ALU.mult))
                    dve.wait_ge(kk_ready, t + 1)
                    then(v.tensor_tensor(lt[s], hb(X + 1), dm[s], ALU.mult))
                    v.tensor_tensor(lt[s], lt[s], per_head(beta, t), ALU.mult).then_inc(lt_ready, 1)
                    dve.wait_ge(qk_ready, t + 1)
                    v.tensor_tensor(at_[s], hb(X + 2), dm[s], ALU.mult).then_inc(at_ready, 1)
                for level in range(LEVELS):
                    for s in range(2):
                        X = 3 * s
                        if level == 0:
                            dve.wait_ge(m_ready[s], LEVELS * tp + 1)
                            v.tensor_tensor(tri[s], over_heads(ident), hb(X), ALU.subtract)
                            v.tensor_tensor(triT[s], over_heads(ident), lo[s], ALU.subtract).then_inc(tri_ready[s], 1)
                            continue
                        dve.wait_ge(p_ready[s], (LEVELS - 1) * tp + level)
                        dve.wait_ge(tri_ready[s], LEVELS * tp + level)
                        if level < LEVELS - 1:
                            v.tensor_tensor(tri[s], tri[s], hb(X + 1), ALU.subtract)
                        v.tensor_tensor(triT[s], triT[s], hb(X + 2), ALU.subtract).then_inc(tri_ready[s], 1)
                for s in range(2):
                    t = 2 * tp + s
                    X = 3 * s
                    for c in range(2):
                        n = 2 * t + c
                        rows = slice(c * CHUNK, (c + 1) * CHUNK)
                        dve.wait_ge(zeroed, 2)
                        dve.wait_ge(vn_ready, n + 1)
                        if n >= 2:
                            dve.wait_ge(og_ready, n - 1)
                        v.tensor_tensor(vnew[c][rows], hb(X + 1)[rows], per_head(beta, t)[rows], ALU.mult).then_inc(vnew_ready, 1)
                        dve.wait_ge(sup_ready, n + 1)
                        if n >= 1:
                            dve.wait_ge(state_ready, n)
                            dve.wait_ge(og_ready, n)
                        for h in range(H):
                            i = c * NG + t * H + h
                            last = v.scalar_tensor_tensor(state[(n + 1) % 2][:, h], state[n % 2][:, h], egl[:, i:i + 1],
                                                          hb(X)[:, h], ALU.mult, ALU.add)
                        last.then_inc(state_ready, 1)

        modps = bank(7)
        h2T, rowsb = work[:, 0:8], work[:, 8:13]
        R_G1, R_GAIN2, R_SH2, R_G2, R_FIN = range(5)
        row_cols = [16, 32, 24, 40]
        w_late = [ring[0], r_h[:, 0:4096], r_h[:, 4096:8192]]
        w_outv = A["w_out"][0].rearrange("(k p) n -> p k n", p=P)
        wout = [t.rearrange("p (k n) -> p k n", k=KD) for t in (ring[0], r_z[:, :])]
        x2 = r_qkv[:, 0:NT * D].rearrange("p (t n) -> p t n", t=NT)
        h2 = r_h[:, :].rearrange("p (t n) -> p t n", t=NT)
        h2_dram = nc.dram_tensor("h2_rows", [S, D], F32).ap()
        rdiag = [ring[2][:, i * HALF:(i + 1) * HALF] for i in range(2)]
        otmp = ring[2][:, 1024:2048]
        E = 64
        GROUPS, PER = 8, 8
        wr = ring[2][:, 2048:2560].rearrange("p (k e) -> p k e", k=KD)
        rbias = ring[2][:, 2560:2624]
        comb = ring[2][:, 2624:3136].rearrange("p (t e) -> p t e", t=NT)
        sel = ring[2][:, 3136:3648].rearrange("p (t e) -> p t e", t=NT)
        scores = [sb(f"scores{i}", E) for i in range(2)]
        biased = ring[2][:, 3648:3712]
        masked = ring[2][:, 3712:3776]
        tops = ring[2][:, 3776:3840]
        emark = ring[2][:, 3840:3904]
        gsum = ring[2][:, 3904:3916]
        gmark = ring[2][:, 3916:3928]
        gtop = ring[2][:, 3928:3936]
        gval = ring[2][:, 3936:3944]
        gpen = ring[2][:, 3944:3952]
        etop = ring[2][:, 3952:3960]
        den = ring[2][:, 3960:3961]
        rden = ring[2][:, 3961:3962]
        BIG = 1e30

        wout_loaded = [sem(f"wout_loaded{i}") for i in range(2)]
        small_loaded = sem("small_loaded")
        mod2_ready = sem("mod2_ready")
        rdiag_ready = sem("rdiag_ready")
        rspread_ready = sem("rspread_ready")
        row_ready = sem("row_ready")
        mix_ready = sem("mix_ready")
        mix_used = sem("mix_used")
        x2_ready = sem("x2_ready")
        ssq2_ready = sem("ssq2_ready")
        std2_ready = sem("std2_ready")
        h2_ready = sem("h2_ready")
        h2_written = sem("h2_written")
        h2T_ready = sem("h2T_ready")
        h2T_stored = sem("h2T_stored")
        logits_ready = sem("logits_ready")
        scores_set = sem("scores_set")
        comb_ready = sem("comb_ready")

        def out_sp(sp):
            sp.wait_ge(o_stored, N_ST)
            for m in range(8):
                if m >= 3:
                    sp.wait_ge(mod2_ready, m - 2)
                sp.dma_start(w_late[m % 3].rearrange("p (k n) -> p k n", k=KD),
                             cols(ada, (4 + m) * HALF, (5 + m) * HALF)).then_inc(ring_loaded[m % 3], 16)
            sp.wait_ge(og_stored, 2 * NT)
            sp.wait_ge(state_ready, 2 * NT)
            sp.dma_start(wr, A["router_w"][0].rearrange("(k p) e -> p k e", p=P)).then_inc(small_loaded, 16)
            sp.dma_start(rbias, A["router_bias"][0].partition_broadcast(P)).then_inc(small_loaded, 16)
            for t in range(NT):
                sp.dma_start(x2[:, t], A["x"][0, t * P:(t + 1) * P, :]).then_inc(x_loaded[t], 16)
            sp.wait_ge(mod2_ready, 7)
            sp.dma_start(wout[0], cols(w_outv, 0, HALF)).then_inc(wout_loaded[0], 16)
            sp.wait_ge(normed, N_JOBS + H)
            sp.dma_start(wout[1], cols(w_outv, HALF, D)).then_inc(wout_loaded[1], 16)
            sp.dma_start(rowsb[:, R_FIN], A["final_norm_w"].partition_broadcast(P)).then_inc(small_loaded, 16)
            for t in range(NT):
                sp.wait_ge(h2_ready, t + 1)
                sp.dma_start(h2_dram[t * P:(t + 1) * P, :], h2[:, t]).then_inc(h2_written, 16)
        def out_pool(pool):
            pass

        def out_pe(pe):
            mm = nc.tensor.matmul
            for h in range(H):
                pe.wait_ge(squares_ready, len(norm_tiles) + h + 1)
                for t in range(NT):
                    last = mm(bank(6)[:, h * NT + t:h * NT + t + 1], sq[:, h % 2, t * P:(t + 1) * P], ones[:, 0:1],
                              start=True, stop=True)
                last.then_inc(sumsq_ready, 1)
            for m in range(8):
                pe.wait_ge(ring_loaded[m % 3], 16 * (len(ring_loads) // 3 + m // 3 + 1))
                w = w_late[m % 3].rearrange("p (k n) -> p k n", k=KD)
                for q in range(4):
                    for k in range(KD):
                        last = mm(modps[:, 4 * m + q:4 * m + q + 1], w[:, k, q * P:(q + 1) * P], csil[:, k:k + 1],
                                  start=(k == 0), stop=(k == KD - 1))
                last.then_inc(mod2_ready, 1)
            for h in range(H):
                pe.wait_ge(diag_ready, N_JOBS + h + 1)
                if h >= 2:
                    pe.wait_ge(normed, N_JOBS + h - 1)
                for half in range(2):
                    last = mm(bank(2 * (h % 2) + half), ones[:, :], diag[:, h % 2, half * HALF:(half + 1) * HALF],
                              start=True, stop=True)
                last.then_inc(spread_ready, 1)
            for i in range(8):
                pe.wait_ge(rdiag_ready, i + 1)
                if i >= 2:
                    pe.wait_ge(row_ready, i - 1)
                mm(bank(4 + i % 2), ones[:, :], rdiag[i % 2], start=True, stop=True).then_inc(rspread_ready, 1)
            pe.wait_ge(normed, N_JOBS + H)
            pe.wait_ge(wout_loaded[0], 16)
            pe.wait_ge(wout_loaded[1], 16)

            def late(t):
                pe.wait_ge(h2_ready, t + 1)
                if t == 0:
                    pe.wait_ge(row_ready, 8)
                if t >= 1:
                    pe.wait_ge(h2T_stored, t)
                for k in range(KD):
                    last = nc.tensor.transpose(pair[2][:, k * P:(k + 1) * P], h2[:, t, k * P:(k + 1) * P], ident)
                last.then_inc(h2T_ready, 1)
                pe.wait_ge(h2T_stored, t + 1)
                pe.wait_ge(small_loaded, 48)
                if t >= 2:
                    pe.wait_ge(scores_set, t - 1)
                for k in range(KD):
                    last = mm(bank(6 + t % 2)[:, 0:E], h2T[:, k, t * P:(t + 1) * P], wr[:, k], start=(k == 0), stop=(k == KD - 1))
                last.then_inc(logits_ready, 1)

            for t in range(NT):
                if t >= 2:
                    pe.wait_ge(mix_used, t - 1)
                for half in range(2):
                    for k in range(KD):
                        o = oT_mla[:, k] if k < H else oT_gdn[:, k - H]
                        last = mm(pair[t % 2][:, half * HALF:(half + 1) * HALF], o[:, t * P:(t + 1) * P], wout[half][:, k],
                                  start=(k == 0), stop=(k == KD - 1))
                last.then_inc(mix_ready, 1)
                if t >= 2:
                    late(t - 2)
            late(NT - 2)
            late(NT - 1)

        def out_act(act):
            do = nc.scalar.activation
            for h in range(H):
                act.wait_ge(og_stored, 2 * NT)
                if h == 0:
                    act.wait_ge(state_ready, 2 * NT)
                    act.wait_ge(at_ready, NT)
                    act.wait_ge(og_ready, 2 * NT)
                if h >= 2:
                    act.wait_ge(sumsq_ready, len(norm_tiles) + h - 1)
                do(sq[:, h % 2], oT_gdn[:, h], ACT.Square).then_inc(squares_ready, 1)
            act.wait_ge(sumsq_ready, len(norm_tiles) + H)
            do(ncol[:, 0:H * NT], bank(6)[:, 0:H * NT], ACT.Sqrt, bias=bias[:, 0:1], scale=1.0 / P).then_inc(ncol_ready, 1)
            for i in range(8):
                act.wait_ge(rspread_ready, i + 1)
                if i == 0:
                    act.wait_ge(normed, N_JOBS + H)
                r, half = i // 2, i % 2
                do(rowsb[:, r, half * HALF:(half + 1) * HALF], bank(4 + i % 2), ACT.Copy).then_inc(row_ready, 1)

            def late(t):
                act.wait_ge(h2T_ready, t + 1)
                do(h2T[:, :, t * P:(t + 1) * P], pair[2][:, :].rearrange("p (k n) -> p k n", k=KD), ACT.Copy)\
                    .then_inc(h2T_stored, 1)
                act.wait_ge(logits_ready, t + 1)
                if t >= 2:
                    act.wait_ge(comb_ready, t - 1)
                do(scores[t % 2][:, :], bank(6 + t % 2)[:, 0:E], ACT.Sigmoid).then_inc(scores_set, 1)

            for t in range(NT):
                act.wait_ge(x2_ready, t + 1)
                if t >= 1:
                    act.wait_ge(h2_ready, t)
                do(h2[:, t], x2[:, t], ACT.Square, accum_out=ssq[:, t:t + 1]).then_inc(ssq2_ready, 1)
                act.wait_ge(ssq2_ready, t + 1)
                do(std[:, t:t + 1], ssq[:, t:t + 1], ACT.Sqrt, bias=bias[:, 0:1], scale=1.0 / D).then_inc(std2_ready, 1)
                if t >= 2:
                    late(t - 2)
            late(NT - 2)
            late(NT - 1)

        def out_dve(dve, then):
            v = nc.vector
            dve.wait_ge(ncol_ready, 4 + 1)
            then(v.reciprocal(rcol[:, 0:H * NT], ncol[:, 0:H * NT]))

            def make_diag(h):
                if h >= 2:
                    dve.wait_ge(spread_ready, N_JOBS + h - 1)
                v.tensor_tensor(diag[:, h % 2].rearrange("p (t c) -> p t c", t=NT),
                                ident.unsqueeze(1).broadcast_to([P, NT, P]),
                                rcol[:, h * NT:(h + 1) * NT].unsqueeze(2).broadcast_to([P, NT, P]),
                                ALU.mult).then_inc(diag_ready, 1)

            make_diag(0)
            for h in range(H):
                if h + 1 < H:
                    make_diag(h + 1)
                dve.wait_ge(spread_ready, N_JOBS + h + 1)
                then(v.scalar_tensor_tensor(oT_gdn[:, h], oT_gdn[:, h], vec[:, V_GN:V_GN + 1], pair[h % 2][:, :], ALU.mult, ALU.mult))
                v.tensor_tensor(oT_gdn[:, h], oT_gdn[:, h], zT[:, h], ALU.mult).then_inc(normed, 1)
            dve.wait_ge(mod2_ready, 8)
            then(v.tensor_tensor(modc[:, 16:48], modps[:, 0:32], vec[:, V_ADAB + 16:V_ADAB + 48], ALU.add))
            then(v.scalar_tensor_tensor(modc[:, 32:40], modc[:, 32:40], 1.0, vec[:, V_N2:V_N2 + KD], ALU.add, ALU.mult))
            for i in range(8):
                if i >= 2:
                    dve.wait_ge(rspread_ready, i - 1)
                c0 = row_cols[i // 2] + 4 * (i % 2)
                v.tensor_tensor(rdiag[i % 2].rearrange("p (t c) -> p t c", t=4), ident.unsqueeze(1).broadcast_to([P, 4, P]),
                                modc[:, c0:c0 + 4].unsqueeze(2).broadcast_to([P, 4, P]), ALU.mult).then_inc(rdiag_ready, 1)
            dve.wait_ge(row_ready, 8)
            v.memset(gsum[:, GROUPS:GROUPS + 4], -BIG)
            then(v.memset(gval[:, 4:8], -BIG))

            def route(t):
                dve.wait_ge(scores_set, t + 1)
                sc = scores[t % 2][:, :]
                then(v.tensor_tensor(biased, sc, rbias, ALU.add))
                for gr in range(GROUPS):
                    ins = v.max(tops[:, gr * 8:(gr + 1) * 8], biased[:, gr * PER:(gr + 1) * PER])
                then(ins)
                best = tops.rearrange("p (g n) -> p g n", g=GROUPS)
                then(v.tensor_tensor(gsum[:, 0:GROUPS].unsqueeze(2), best[:, :, 0:1], best[:, :, 1:2], ALU.add))
                then(v.max(gtop, gsum[:, 0:GROUPS]))
                then(v.tensor_copy(gval[:, 0:4], gtop[:, 0:4]))
                then(v.match_replace(gmark, gval, gsum, -2 * BIG))
                then(v.tensor_tensor(gpen, gmark[:, 0:GROUPS], gsum[:, 0:GROUPS], ALU.not_equal))
                then(v.tensor_scalar(gpen, gpen, 1.0, BIG, ALU.subtract, ALU.mult))
                then(v.tensor_tensor(masked.rearrange("p (g n) -> p g n", g=GROUPS), biased.rearrange("p (g n) -> p g n", g=GROUPS),
                                     gpen.unsqueeze(2).broadcast_to([P, GROUPS, PER]), ALU.add))
                then(v.max(etop, masked))
                then(v.match_replace(emark, etop, masked, -2 * BIG))
                then(v.tensor_tensor(sel[:, t], emark, masked, ALU.not_equal))
                then(v.scalar_tensor_tensor(comb[:, t], sc, 1.0, sel[:, t], ALU.mult, ALU.mult, accum_out=den))
                then(v.reciprocal(rden, den))
                v.tensor_scalar(comb[:, t], comb[:, t], rden, 2.5, ALU.mult, ALU.mult).then_inc(comb_ready, 1)

            for t in range(NT):
                dve.wait_ge(mix_ready, t + 1)
                dve.wait_ge(x_loaded[t], 32)
                if t >= 1:
                    dve.wait_ge(x2_ready, t)
                v.tensor_tensor(otmp, pair[t % 2][:, :], rowsb[:, R_G1], ALU.mult).then_inc(mix_used, 1)
                dve.wait_ge(mix_used, t + 1)
                v.tensor_tensor(x2[:, t], x2[:, t], otmp, ALU.add).then_inc(x2_ready, 1)
                dve.wait_ge(std2_ready, t + 1)
                then(v.reciprocal(rstd[:, t:t + 1], std[:, t:t + 1]))
                then(v.scalar_tensor_tensor(h2[:, t], x2[:, t], rstd[:, t:t + 1], rowsb[:, R_GAIN2], ALU.mult, ALU.mult))
                v.tensor_tensor(h2[:, t], h2[:, t], rowsb[:, R_SH2], ALU.add).then_inc(h2_ready, 1)
                if t >= 2:
                    route(t - 2)
            route(NT - 2)
            route(NT - 1)

        NBLK = S * 8 // P + E
        F = 256
        FT = F // P
        OUT_OF_RANGE = 1 << 20
        tables = r_work[:, 8 * S:11 * S]

        def table(at, width):
            return tables[:, at:at + width]

        latec = table(0, P + NT)
        iota_row, tok_id = latec[:, 0:P], latec[:, P:P + NT]
        pre = table(160, (NT + 2) * E)
        slotv = table(800, NT * E)
        slots8 = table(1312, NT * 8)
        wts = table(1376, NT * 8)
        entry = table(1440, NT * 8 * 2).bitcast(U32)
        rows_idx = table(1568, NT * 8).bitcast(U32)
        tab = table(1632, 2 * P).bitcast(U32)
        block_e = table(1888, P).bitcast(I32)
        nbrep = table(2016, P)
        ge = table(2144, P)
        misc = table(2272, 8)
        ncount, nb, endcol = misc[:, 0:1], misc[:, 1:2], misc[:, 2:3]
        starts = table(2280, E)
        quot = table(2344, NT * 8)
        s128 = table(2408, NT * 8)
        junk = table(2472, E)
        tab_init = table(2560, 2 * P).bitcast(U32)
        strict = consts[:, C_STRICT:C_STRICT + P]
        table_dram = nc.dram_tensor("slot_table", [P * NBLK, 2], U32).ap()
        acc_dram = nc.dram_tensor("moe_rows", [S, D], F32).ap()

        gu = [r_h[:, 4096 * i:4096 * (i + 1)] for i in range(2)]
        wd = [r_z[:, 2048 * i:2048 * (i + 1)].rearrange("p (j n) -> p j n", j=FT) for i in range(2)]
        sh_gu, sh_wd = ring[1], wd[1]
        xb = [r_qkv[:, (8 + i) * S:(9 + i) * S] for i in range(2)]
        yb = [r_qkv[:, (10 + i) * S:(11 + i) * S] for i in range(2)]
        xbT = [ring[0][:, i * S:(i + 1) * S].rearrange("p (k n) -> p k n", k=KD) for i in range(2)]
        hid = [ring[0][:, 2048 + i * F:2048 + (i + 1) * F] for i in range(2)]
        hidT = [ring[0][:, 2560 + i * F:2560 + (i + 1) * F].rearrange("p (j n) -> p j n", j=FT) for i in range(2)]
        sg = [ring[0][:, 3072 + i * F:3072 + (i + 1) * F] for i in range(2)]
        gidx = [sb(f"gidx{i}", 1, U32) for i in range(2)]
        sidx = [sb(f"sidx{i}", 1, U32) for i in range(2)]
        settled = sb("settled", 1)
        wcol = [sb(f"wcol{i}", 1) for i in range(2)]

        latec_loaded = sem("latec_loaded")
        pre_ready = sem("pre_ready")
        rank_ready = sem("rank_ready")
        nb_ready = sem("nb_ready")
        starts_ready = sem("starts_ready")
        ge_ready = sem("ge_ready")
        be_sum = sem("be_sum")
        be_ready = sem("be_ready")
        entry_ready = sem("entry_ready")
        init_ready = sem("init_ready")
        init_written = sem("init_written")
        scattered = sem("scattered")
        tab_loaded = sem("tab_loaded")
        shw_loaded = sem("shw_loaded")
        shgu_ready = sem("shgu_ready")
        shsg_ready = sem("shsg_ready")
        shh_ready = sem("shh_ready")
        shhT_ready = sem("shhT_ready")
        shhT_stored = sem("shhT_stored")
        shy_ready = sem("shy_ready")
        shy_stored = sem("shy_stored")
        acc_written = [sem(f"acc_written{i}") for i in range(2)]
        gu_loaded = [sem(f"gu_loaded{i}") for i in range(2)]
        wd_loaded = [sem(f"wd_loaded{i}") for i in range(2)]
        xb_zeroed = sem("xb_zeroed")
        gidx_ready = sem("gidx_ready")
        sidx_ready = sem("sidx_ready")
        wcol_ready = sem("wcol_ready")
        xb_loaded = [sem(f"xb_loaded{i}") for i in range(2)]
        xbT_ready = sem("xbT_ready")
        xbT_act = sem("xbT_act")
        xbT_dve = sem("xbT_dve")
        gu_ready = sem("gu_ready")
        sg_ready = sem("sg_ready")
        hid_ready = sem("hid_ready")
        hidT_ready = sem("hidT_ready")
        hidT_stored = sem("hidT_stored")
        y_ready = sem("y_ready")
        y_act = sem("y_act")
        y_dve = sem("y_dve")
        y_added = sem("y_added")
        x3_ready = sem("x3_ready")
        ssq3_ready = sem("ssq3_ready")
        std3_ready = sem("std3_ready")
        out_ready = sem("out_ready")
        out_written = sem("out_written")
        gate_e = A["exp_w_gate"][0].rearrange("e (p k) f -> e p (k f)", k=KD)
        up_e = A["exp_w_up"][0].rearrange("e (p k) f -> e p (k f)", k=KD)
        down_e = A["exp_w_down"][0].rearrange("e (p j) n -> e p (j n)", j=FT)

        def halves(w):
            return w.rearrange("p (u k f) -> p k u f", u=2, k=KD)

        def moe_sp(sp):
            sp.wait_ge(mix_ready, NT)
            sp.dma_start(sh_gu[:, 0:2048].rearrange("p (k f) -> p k f", k=KD),
                         A["sh_w_gate"][0].rearrange("(k p) f -> p k f", p=P)).then_inc(shw_loaded, 16)
            sp.dma_start(sh_gu[:, 2048:4096].rearrange("p (k f) -> p k f", k=KD),
                         A["sh_w_up"][0].rearrange("(k p) f -> p k f", p=P)).then_inc(shw_loaded, 16)
            sp.dma_start(sh_wd, A["sh_w_down"][0].rearrange("(j p) n -> p j n", p=P)).then_inc(shw_loaded, 16)
            sp.wait_ge(h2_ready, NT)
            sp.dma_start(latec, A["late_constants"]).then_inc(latec_loaded, 16)
            sp.wait_ge(init_ready, 1)
            sp.dma_start(table_dram.rearrange("(p b) n -> p (b n)", p=P), tab_init).then_inc(init_written, 16)
            for t in range(NT):
                sp.wait_ge(shy_stored, t + 1)
                sp.dma_start(acc_dram[t * P:(t + 1) * P, :], yb[t % 2]).then_inc(acc_written[t % 2], 16)
            sp.wait_ge(scattered, 16 * NT * 8)
            sp.dma_start(tab, table_dram.rearrange("(p b) n -> p (b n)", p=P)).then_inc(tab_loaded, 16)
            sp.wait_ge(be_ready, 1)
            sp.wait_ge(h2_written, 16 * NT)
            sp.wait_ge(h2T_ready, NT)
            sp.wait_ge(shy_ready, NT)

            def load(b, i, before):
                e = sp.value_load(block_e[0:1, bass.ds(b, 1)], min_val=0, max_val=E - 1)
                if before is not None:
                    sp.wait_ge(gu_ready, before)
                sp.dma_start(gu[i][:, 0:2048], gate_e[bass.ds(e, 1)].rearrange("e p n -> p (e n)")).then_inc(gu_loaded[i], 16)
                sp.dma_start(gu[i][:, 2048:4096], up_e[bass.ds(e, 1)].rearrange("e p n -> p (e n)")).then_inc(gu_loaded[i], 16)
                if before is not None:
                    sp.wait_ge(y_ready, before)
                sp.dma_start(wd[i].rearrange("p j n -> p (j n)"), down_e[bass.ds(e, 1)].rearrange("e p n -> p (e n)"))\
                    .then_inc(wd_loaded[i], 16)

            for i in range(2):
                load(i, i, None)
            with sp.Fori(1, NBLK // 2) as it:
                for i in range(2):
                    load(2 * it + i, i, 2 * it + i - 1)
            sp.wait_ge(y_added, 16 * NBLK)
            for t in range(NT):
                sp.dma_start(r_h[:, t * S:(t + 1) * S], acc_dram[t * P:(t + 1) * P, :]).then_inc(x_loaded[t], 16)
            for t in range(NT):
                sp.wait_ge(out_ready, t + 1)
                sp.dma_start(out[0, t * P:(t + 1) * P, :], r_h[:, t * S:(t + 1) * S]).then_inc(out_written, 16)
            sp.wait_ge(out_written, 16 * NT)

        def moe_pool(pool):
            pool.wait_ge(latec_loaded, 16)
            nc.gpsimd.memset(tab_init, OUT_OF_RANGE).then_inc(init_ready, 1)
            pool.wait_ge(entry_ready, 1)
            pool.wait_ge(init_written, 16)
            for i in range(NT * 8):
                nc.gpsimd.indirect_dma_start(out=table_dram, out_offset=bass.IndirectOffsetOnAxis(ap=rows_idx[:, i:i + 1], axis=0),
                                             in_=entry[:, 2 * i:2 * i + 2], in_offset=None).then_inc(scattered, 16)
            pool.wait_ge(tab_loaded, 16)
            for i in range(2):
                pool.wait_ge(acc_written[i], 8 * NT)
            for i in range(2):
                nc.gpsimd.memset(xb[i], 0.0).then_inc(xb_zeroed, 1)
            pool.wait_ge(xb_zeroed, 2)
            pool.wait_ge(h2_written, 16 * NT)

            def settle():
                nc.gpsimd.tensor_tensor(settled[:, :], ones[:, 0:1], ones[:, 0:1], ALU.mult)

            def gather(b, i, before):
                if before is not None:
                    pool.wait_ge(xbT_ready, before)
                nc.gpsimd.tensor_copy(gidx[i][:, :], tab[:, bass.ds(2 * b, 1)]).then_inc(gidx_ready, 1)
                pool.wait_ge(gidx_ready, b + 1)
                settle()
                nc.gpsimd.indirect_dma_start(out=xb[i], out_offset=None, in_=h2_dram,
                                             in_offset=bass.IndirectOffsetOnAxis(ap=gidx[i][:, :], axis=0),
                                             bounds_check=S - 1, oob_is_err=False).then_inc(xb_loaded[i], 16)

            def weights_col(b, i, before):
                if before is not None:
                    pool.wait_ge(hid_ready, before)
                nc.gpsimd.tensor_copy(wcol[i][:, :], tab.bitcast(F32)[:, bass.ds(2 * b + 1, 1)]).then_inc(wcol_ready, 1)

            def scatter(b, i, before):
                if before is not None:
                    pool.wait_ge(y_added, 16 * before)
                nc.gpsimd.tensor_copy(sidx[i][:, :], tab[:, bass.ds(2 * b, 1)]).then_inc(sidx_ready, 1)
                pool.wait_ge(sidx_ready, b + 1)
                pool.wait_ge(y_act, b + 1)
                pool.wait_ge(y_dve, b + 1)
                settle()
                nc.gpsimd.indirect_dma_start(out=acc_dram, out_offset=bass.IndirectOffsetOnAxis(ap=sidx[i][:, :], axis=0),
                                             in_=yb[i], in_offset=None, bounds_check=S - 1, oob_is_err=False,
                                             compute_op=ALU.add).then_inc(y_added, 16)

            for i in range(2):
                gather(i, i, None)
                weights_col(i, i, None)
            for i in range(2):
                gather(2 + i, i, 1 + i)
                weights_col(2 + i, i, 1 + i)
                scatter(i, i, None if i == 0 else 1)
            with pool.Fori(1, NBLK // 2 - 1) as it:
                for i in range(2):
                    gather(2 * it + i + 2, i, 2 * it + i + 1)
                    weights_col(2 * it + i + 2, i, 2 * it + i + 1)
                    scatter(2 * it + i, i, 2 * it + i)
            for i in range(2):
                scatter(NBLK - 2 + i, i, NBLK - 2 + i)

        def moe_pe(pe):
            mm = nc.tensor.matmul
            pe.wait_ge(pre_ready, 1)
            for t in range(NT):
                mm(bank(0)[:, t * E:(t + 1) * E], strict, sel[:, t], start=True, stop=False)
                mm(bank(0)[:, t * E:(t + 1) * E], ones[:, :], pre[:, t * E:(t + 1) * E], start=False, stop=True)
            mm(bank(1)[:, 0:1], pre[:, NT * E:(NT + 2) * E], ones[:, 0:1], start=True, stop=True).then_inc(rank_ready, 1)
            pe.wait_ge(nb_ready, 1)
            mm(bank(1)[:, E:2 * E], nbrep, strict[:, 0:E], start=True, stop=True)
            mm(bank(1)[:, 2 * E:2 * E + 1], strict, nb, start=True, stop=False)
            mm(bank(1)[:, 2 * E:2 * E + 1], ident, nb, start=False, stop=True).then_inc(starts_ready, 1)
            pe.wait_ge(ge_ready, 1)
            first_rows = consts[:, C_ONEB:C_ONEB + 1].broadcast_to([P, P])
            mm(bank(1)[:, 0:P], first_rows, ge, start=True, stop=True).then_inc(be_sum, 1)

            def sh_out(t):
                pe.wait_ge(shh_ready, t + 1)
                if t >= 1:
                    pe.wait_ge(shhT_stored, t)
                for j in range(FT):
                    last = nc.tensor.transpose(bank(4)[:, j * P:(j + 1) * P], hid[t % 2][:, j * P:(j + 1) * P], ident)
                last.then_inc(shhT_ready, 1)
                pe.wait_ge(shhT_stored, t + 1)
                if t >= 1:
                    pe.wait_ge(shy_stored, t)
                for half in range(2):
                    for j in range(FT):
                        last = mm(pair[3][:, half * HALF:(half + 1) * HALF], hidT[t % 2][:, j],
                                  sh_wd[:, j, half * HALF:(half + 1) * HALF], start=(j == 0), stop=(j == FT - 1))
                last.then_inc(shy_ready, 1)

            pe.wait_ge(shw_loaded, 48)
            pe.wait_ge(scores_set, NT)
            for t in range(NT):
                if t >= 2:
                    pe.wait_ge(shh_ready, t - 1)
                for k in range(KD):
                    last = mm(bank(2 + t % 2), h2T[:, k, t * P:(t + 1) * P], halves(sh_gu)[:, k], start=(k == 0), stop=(k == KD - 1))
                last.then_inc(shgu_ready, 1)
                if t >= 1:
                    sh_out(t - 1)
            sh_out(NT - 1)
            def x_to_features(b, i, before):
                pe.wait_ge(xb_loaded[i], 16 * before[0])
                if before[1] is not None:
                    pe.wait_ge(xbT_act, before[1])
                    pe.wait_ge(xbT_dve, before[1])
                for k in range(KD):
                    last = nc.tensor.transpose(pair[0][:, k * P:(k + 1) * P], xb[i].rearrange("p (q k) -> p k q", k=KD)[:, k], ident)
                last.then_inc(xbT_ready, 1)

            def gate_up(b, i, loads, before):
                pe.wait_ge(xbT_act, b + 1)
                pe.wait_ge(xbT_dve, b + 1)
                pe.wait_ge(gu_loaded[i], 32 * loads)
                if before is not None:
                    pe.wait_ge(hid_ready, before)
                for k in range(KD):
                    last = mm(bank(2 + i), xbT[i][:, k], halves(gu[i])[:, k], start=(k == 0), stop=(k == KD - 1))
                last.then_inc(gu_ready, 1)

            def down(b, i, loads, before):
                pe.wait_ge(hid_ready, b + 1)
                if before is not None:
                    pe.wait_ge(hidT_stored, before)
                for j in range(FT):
                    last = nc.tensor.transpose(bank(4)[:, j * P:(j + 1) * P], hid[i].rearrange("p (q j) -> p j q", j=FT)[:, j], ident)
                last.then_inc(hidT_ready, 1)
                pe.wait_ge(hidT_stored, b + 1)
                pe.wait_ge(wd_loaded[i], 16 * loads)
                if before is not None:
                    pe.wait_ge(y_act, before)
                    pe.wait_ge(y_dve, before)
                for half in range(2):
                    for j in range(FT):
                        last = mm(pair[3][:, half * HALF:(half + 1) * HALF], hidT[i][:, j],
                                  wd[i][:, j, half * HALF:(half + 1) * HALF], start=(j == 0), stop=(j == FT - 1))
                last.then_inc(y_ready, 1)

            pe.wait_ge(be_ready, 1)
            pe.wait_ge(shhT_stored, NT)
            pe.wait_ge(shy_stored, NT)
            x_to_features(0, 0, (1, None))
            gate_up(0, 0, 1, None)
            x_to_features(1, 1, (1, 1))
            gate_up(1, 1, 1, None)
            x_to_features(2, 0, (2, 2))
            down(0, 0, 1, None)
            with pe.Fori(1, NBLK // 2 - 1) as it:
                for i in range(2):
                    b = 2 * it + i
                    gate_up(b, i, it + 1, b - 1)
                    x_to_features(b + 1, 1 - i, (it + 1 + i, b + 1))
                    down(b - 1, 1 - i, it + i, b - 1)
            last_b = NBLK - 2
            gate_up(last_b, 0, NBLK // 2, last_b - 1)
            x_to_features(last_b + 1, 1, (NBLK // 2, last_b + 1))
            down(last_b - 1, 1, NBLK // 2 - 1, last_b - 1)
            gate_up(last_b + 1, 1, NBLK // 2, last_b)
            down(last_b, 0, NBLK // 2, last_b)
            down(last_b + 1, 1, NBLK // 2, last_b + 1)

        def moe_act(act):
            do = nc.scalar.activation

            def sh_late(t):
                act.wait_ge(shhT_ready, t + 1)
                do(hidT[t % 2], bank(4)[:, 0:F].rearrange("p (j n) -> p j n", j=FT), ACT.Copy).then_inc(shhT_stored, 1)
                act.wait_ge(shy_ready, t + 1)
                if t >= 2:
                    act.wait_ge(acc_written[t % 2], 16 * (t // 2))
                do(yb[t % 2], pair[3][:, :], ACT.Copy).then_inc(shy_stored, 1)

            for t in range(NT):
                act.wait_ge(shgu_ready, t + 1)
                if t >= 2:
                    act.wait_ge(shh_ready, t - 1)
                do(sg[t % 2], bank(2 + t % 2)[:, 0:F], ACT.Silu).then_inc(shsg_ready, 1)
                if t >= 1:
                    sh_late(t - 1)
            sh_late(NT - 1)
            def x_half(b, i, before):
                act.wait_ge(xbT_ready, b + 1)
                if before is not None:
                    act.wait_ge(gu_ready, before)
                do(xbT[i][:, 0:KD // 2], pair[0][:, 0:HALF].rearrange("p (k n) -> p k n", k=KD // 2), ACT.Copy).then_inc(xbT_act, 1)

            def silu_gate(b, i, before):
                act.wait_ge(gu_ready, b + 1)
                if before is not None:
                    act.wait_ge(hid_ready, before)
                do(sg[i], bank(2 + i)[:, 0:F], ACT.Silu).then_inc(sg_ready, 1)

            def out_half(b, i, before):
                act.wait_ge(hidT_ready, b + 1)
                if before is not None:
                    act.wait_ge(y_ready, before)
                do(hidT[i], bank(4)[:, 0:F].rearrange("p (j n) -> p j n", j=FT), ACT.Copy).then_inc(hidT_stored, 1)
                act.wait_ge(y_ready, b + 1)
                if before is not None:
                    act.wait_ge(y_added, 16 * before)
                do(yb[i][:, 0:HALF], pair[3][:, 0:HALF], ACT.Copy).then_inc(y_act, 1)

            for i in range(2):
                act.wait_ge(acc_written[i], 8 * NT)
            x_half(0, 0, None)
            silu_gate(0, 0, None)
            x_half(1, 1, None)
            silu_gate(1, 1, None)
            x_half(2, 0, 1)
            out_half(0, 0, None)
            silu_gate(2, 0, 1)
            x_half(3, 1, 2)
            out_half(1, 1, None)
            silu_gate(3, 1, 2)
            x_half(4, 0, 3)
            out_half(2, 0, 1)
            with act.Fori(2, NBLK // 2 - 1) as it:
                for i in range(2):
                    b = 2 * it + i
                    silu_gate(b, i, b - 1)
                    x_half(b + 1, 1 - i, b)
                    out_half(b - 1, 1 - i, b - 2)
            n = NBLK - 2
            silu_gate(n, 0, n - 1)
            x_half(n + 1, 1, n)
            out_half(n - 1, 1, n - 2)
            silu_gate(n + 1, 1, n)
            out_half(n, 0, n - 1)
            out_half(n + 1, 1, n)
            for t in range(NT):
                act.wait_ge(x3_ready, t + 1)
                do(r_h[:, t * S:(t + 1) * S], x2[:, t], ACT.Square, accum_out=ssq[:, t:t + 1]).then_inc(ssq3_ready, 1)
                act.wait_ge(ssq3_ready, t + 1)
                do(std[:, t:t + 1], ssq[:, t:t + 1], ACT.Sqrt, bias=bias[:, 0:1], scale=1.0 / D).then_inc(std3_ready, 1)

        def moe_dve(dve, then):
            v = nc.vector
            dve.wait_ge(h2_ready, NT)
            dve.wait_ge(latec_loaded, 16)
            v.memset(pre[:, 0:E], 0.0)
            then(v.memset(pre[:, (NT + 1) * E:(NT + 2) * E], 0.0))
            for t in range(NT):
                ins = v.tensor_tensor(pre[:, (t + 1) * E:(t + 2) * E], pre[:, t * E:(t + 1) * E], sel[:, t], ALU.add)
                if t < NT - 1:
                    then(ins)
            ins.then_inc(pre_ready, 1)
            dve.wait_ge(rank_ready, 1)
            floor_shift = 1.0 / (2 * P) - 0.5
            then(v.tensor_scalar(ncount, bank(1)[:, 0:1], 1.0 / P, (P - 1.0) / P + floor_shift, ALU.mult, ALU.add))
            then(v.tensor_scalar(ncount, ncount, ROUND, None, ALU.add))
            then(v.tensor_scalar(nb, ncount, ROUND, None, ALU.subtract))
            v.tensor_scalar(nbrep, ones[:, :], nb, None, ALU.mult).then_inc(nb_ready, 1)
            dve.wait_ge(starts_ready, 1)
            then(v.tensor_copy(endcol, bank(1)[:, 2 * E:2 * E + 1]))
            then(v.tensor_copy(starts, bank(1)[:, E:2 * E]))
            v.tensor_scalar(ge, iota_row, endcol, None, ALU.is_ge).then_inc(ge_ready, 1)
            sv = slotv.rearrange("p (t e) -> p t e", t=NT)
            selv = sel
            then(v.scalar_tensor_tensor(sv, starts.unsqueeze(1).broadcast_to([P, NT, E]), float(P),
                                        bank(0).rearrange("p (t e) -> p t e", t=NT), ALU.mult, ALU.add))
            then(v.scalar_tensor_tensor(sv, sv, 1.0, selv, ALU.add, ALU.mult))
            then(v.tensor_scalar(slotv, slotv, 1.0, None, ALU.subtract))
            dve.wait_ge(be_sum, 1)
            v.tensor_scalar(block_e, bank(1)[:, 0:P], E - 1.0, None, ALU.min).then_inc(be_ready, 1)
            for t in range(NT):
                then(v.max(slots8[:, 8 * t:8 * t + 8], sv[:, t]))
            for i in range(NT * 8):
                then(v.scalar_tensor_tensor(junk, sv[:, i // 8], slots8[:, i:i + 1], comb[:, i // 8], ALU.is_equal, ALU.mult,
                                            accum_out=wts[:, i:i + 1]))
            then(v.tensor_scalar(quot, slots8, 1.0 / P, floor_shift, ALU.mult, ALU.add))
            then(v.tensor_scalar(quot, quot, ROUND, None, ALU.add))
            then(v.tensor_scalar(quot, quot, ROUND, None, ALU.subtract))
            then(v.tensor_scalar(s128, slots8, float(NBLK), None, ALU.mult))
            then(v.scalar_tensor_tensor(s128, quot, 1.0 - P * NBLK, s128, ALU.mult, ALU.add))
            then(v.tensor_copy(rows_idx, s128))
            en = entry.rearrange("p (i n) -> p i n", n=2)
            then(v.tensor_copy(en[:, :, 0].rearrange("p (t i) -> p t i", i=8), tok_id.unsqueeze(2).broadcast_to([P, NT, 8])))
            v.tensor_copy(en[:, :, 1].bitcast(F32), wts).then_inc(entry_ready, 1)
            for t in range(NT):
                dve.wait_ge(shsg_ready, t + 1)
                if t >= 2:
                    dve.wait_ge(shhT_ready, t - 1)
                v.tensor_tensor(hid[t % 2], bank(2 + t % 2)[:, F:2 * F], sg[t % 2], ALU.mult).then_inc(shh_ready, 1)
            def x_half(b, i, before):
                dve.wait_ge(xbT_ready, b + 1)
                if before is not None:
                    dve.wait_ge(gu_ready, before)
                v.tensor_copy(xbT[i][:, KD // 2:KD], pair[0][:, HALF:2 * HALF].rearrange("p (k n) -> p k n", k=KD // 2))\
                    .then_inc(xbT_dve, 1)

            def hidden(b, i, before):
                dve.wait_ge(sg_ready, b + 1)
                dve.wait_ge(wcol_ready, b + 1)
                if before is not None:
                    dve.wait_ge(hidT_ready, before)
                v.scalar_tensor_tensor(hid[i], bank(2 + i)[:, F:2 * F], wcol[i][:, :], sg[i], ALU.mult, ALU.mult)\
                    .then_inc(hid_ready, 1)

            def out_half(b, i, before):
                dve.wait_ge(y_ready, b + 1)
                if before is not None:
                    dve.wait_ge(y_added, 16 * before)
                v.tensor_copy(yb[i][:, HALF:2 * HALF], pair[3][:, HALF:2 * HALF]).then_inc(y_dve, 1)

            dve.wait_ge(shhT_ready, NT)
            for i in range(2):
                dve.wait_ge(acc_written[i], 8 * NT)
            x_half(0, 0, None)
            hidden(0, 0, None)
            x_half(1, 1, None)
            hidden(1, 1, None)
            x_half(2, 0, 1)
            out_half(0, 0, None)
            hidden(2, 0, 1)
            x_half(3, 1, 2)
            out_half(1, 1, None)
            hidden(3, 1, 2)
            x_half(4, 0, 3)
            out_half(2, 0, 1)
            with dve.Fori(2, NBLK // 2 - 1) as it:
                for i in range(2):
                    b = 2 * it + i
                    hidden(b, i, b - 1)
                    x_half(b + 1, 1 - i, b)
                    out_half(b - 1, 1 - i, b - 2)
            n = NBLK - 2
            hidden(n, 0, n - 1)
            x_half(n + 1, 1, n)
            out_half(n - 1, 1, n - 2)
            hidden(n + 1, 1, n)
            out_half(n, 0, n - 1)
            out_half(n + 1, 1, n)
            for t in range(NT):
                acc = r_h[:, t * S:(t + 1) * S]
                dve.wait_ge(x_loaded[t], 48)
                then(v.tensor_tensor(acc, acc, rowsb[:, R_G2], ALU.mult))
                v.tensor_tensor(x2[:, t], x2[:, t], acc, ALU.add).then_inc(x3_ready, 1)
                dve.wait_ge(std3_ready, t + 1)
                then(v.reciprocal(rstd[:, t:t + 1], std[:, t:t + 1]))
                v.scalar_tensor_tensor(acc, x2[:, t], rstd[:, t:t + 1], rowsb[:, R_FIN], ALU.mult, ALU.mult).then_inc(out_ready, 1)


        block = ctx.enter_context(nc.Block())

        @block.sync
        def _(sp):
            for dst, src in setup_loads:
                sp.dma_start(dst, src).then_inc(setup_loaded, 16)
            for n, src in enumerate(ring_loads):
                if n >= 3:
                    if n - 3 < 4:
                        sp.wait_ge(mod_ready, n - 2)
                    else:
                        sp.wait_ge(proj_ready, last_group(n - 3) + 1)
                sp.dma_start(slot(n), src).then_inc(ring_loaded[n % 3], 16)
                if n == 1:
                    for t in range(NT):
                        sp.dma_start(x_in[:, t], A["x"][0, t * P:(t + 1) * P, :]).then_inc(x_loaded[t], 16)
            out_sp(sp)
            moe_sp(sp)
        @block.gpsimd
        def _(pool):
            nc.gpsimd.memset(ones[:, :], 1.0)
            nc.gpsimd.memset(bias[:, 0:1], EPS)
            nc.gpsimd.memset(bias[:, 1:2], P * EPS)
            nc.gpsimd.memset(bias[:, 2:3], 1.0)
            nc.gpsimd.memset(bias[:, 3:4], 0.0).then_inc(bias_set, 1)
            gdn_pool(pool)
            out_pool(pool)
            moe_pool(pool)

        @block.tensor
        def _(pe):
            mm = nc.tensor.matmul
            pe.wait_ge(setup_loaded, N_SETUP)
            nc.tensor.transpose(bank(0)[:, 0:NVEC], vecrows[0:NVEC, :], ident[0:NVEC, 0:NVEC]).then_inc(vecT_ready, 1)
            pe.wait_ge(csil_ready, 1)
            for n in range(4):
                pe.wait_ge(ring_loaded[n % 3], 16 * (n // 3 + 1))
                for q in range(4):
                    for k in range(KD):
                        last = mm(bank(1)[:, 4 * n + q:4 * n + q + 1], slot(n)[:, k, q * P:(q + 1) * P],
                                  csil[:, k:k + 1], start=(k == 0), stop=(k == KD - 1))
                last.then_inc(mod_ready, 1)
            for t in range(NT):
                pe.wait_ge(xn_ready, t + 1)
                if t >= 2:
                    pe.wait_ge(hT_act, t - 1)
                    pe.wait_ge(hT_dve, t - 1)
                for k in range(KD):
                    last = nc.tensor.transpose(pair[2 + t % 2][:, k * P:(k + 1) * P], x_in[:, t, k * P:(k + 1) * P], ident)
                last.then_inc(xT_ready, 1)
            pe.wait_ge(hT_act, NT)
            pe.wait_ge(hT_dve, NT)

            def project(i):
                mms, dst, func, load = groups[i]
                if load is not None:
                    pe.wait_ge(ring_loaded[load % 3], 16 * (load // 3 + 1))
                if i >= 4:
                    pe.wait_ge(proj_stored, i - 3)
                if i == G_KPE or i == G_LAT:
                    pe.wait_ge(wpe_ready, 1 + (i == G_LAT))
                if i == G_AB:
                    for t in range(NT):
                        for k in range(KD):
                            last = mm(bank(i % 4)[:, 8 * t:8 * t + 8], hT[:, k, t * P:(t + 1) * P],
                                      wab[:, 8 * k:8 * k + 8], start=(k == 0), stop=(k == KD - 1))
                else:
                    for k, (w, src) in enumerate(mms):
                        last = mm(bank(i % 4), w, src, start=(k == 0), stop=(k == len(mms) - 1))
                last.then_inc(proj_ready, 1)

            for i in range(G_LAT):
                project(i)
            for idx, (n, k, of, src) in enumerate(norm_tiles):
                pe.wait_ge(squares_ready, idx + 1)
                for t in range(NT):
                    last = mm(bank(4)[:, n * NT + t:n * NT + t + 1], sq[:, idx % 2, t * P:(t + 1) * P], ones[:, 0:1],
                              start=(idx == 0 and t == 0), stop=(k == of - 1), skip_group_check=True)
                last.then_inc(sumsq_ready, 1)
            for n in range(N_JOBS):
                pe.wait_ge(diag_ready, n + 1)
                if n >= 2:
                    pe.wait_ge(normed, n - 1)
                for half in range(2):
                    last = mm(bank(4 + 2 * (n % 2) + half), ones[:, :], diag[:, n % 2, half * HALF:(half + 1) * HALF],
                              start=True, stop=True)
                last.then_inc(spread_ready, 1)
            pe.wait_ge(g_ready, 1)
            pe.wait_ge(normed, N_JOBS)
            NG = NT * H
            mm(bank(4)[:, 0:NG], upper, g[:, :], start=True, stop=True)
            mm(bank(4)[:, NG:2 * NG], consts[:, C_ONEB:C_ONEB + P], g[:, :], start=True, stop=True)
            for c in range(2):
                in_chunk = consts[:, C_ONEB + c * CHUNK:C_ONEB + c * CHUNK + 1].broadcast_to([P, P])
                last = mm(bank(4)[:, (2 + c) * NG:(3 + c) * NG], in_chunk, g[:, :], start=True, stop=True)
            last.then_inc(gcum_ready, 1)
            for i in range(G_LAT, N_GROUPS):
                project(i)
            pe.wait_ge(roped, 3)
            pe.wait_ge(proj_stored, N_GROUPS)
            for a in range(N_ST + 2):
                if a < N_ST:
                    i, h = score_tiles[a]
                    q_at = slice(i * P, (i + 1) * P)
                    r = (h % 2) * ROPE
                    if a >= 2:
                        pe.wait_ge(exp_ready, a - 1)
                    keys = (i + 1) * P
                    for at in range(0, keys, HALF):
                        to = min(at + HALF, keys)
                        s = pair[a % 2][:, at:to]
                        mm(s, qT[:, h, q_at], kT[:, h, at:to], start=True, stop=False)
                        last = mm(s, qpe[r:r + ROPE, h // 2, q_at], kpe[r:r + ROPE, at:to], start=False, stop=True)
                    last.then_inc(scores_ready, 1)
                if 1 <= a <= N_ST:
                    b = a - 1
                    pe.wait_ge(prob_ready, b + 1)
                    if b >= 1:
                        pe.wait_ge(probT_stored, b)
                    for j in range(score_tiles[b][0] + 1):
                        last = nc.tensor.transpose(pair[2][:, j * P:(j + 1) * P], prob[:, b % 2, j * P:(j + 1) * P], ident)
                    last.then_inc(probT_ready, 1)
                if a >= 2:
                    b = a - 2
                    i, h = score_tiles[b]
                    pe.wait_ge(probT_stored, b + 1)
                    if b >= 2:
                        pe.wait_ge(o_stored, b - 1)
                    for j in range(i + 1):
                        last = mm(bank(6 + b % 2)[:, 0:P], v_tok[:, j, h * P:(h + 1) * P], probT[:, b % 2, j * P:(j + 1) * P],
                                  start=(j == 0), stop=(j == i))
                    last.then_inc(pv_ready, 1)
            gdn_pe(pe)
            out_pe(pe)
            moe_pe(pe)

        @block.scalar
        def _(act):
            do = nc.scalar.activation
            act.wait_ge(vec_ready, 1)
            act.wait_ge(bias_set, 1)
            do(csil[:, :], vec[:, V_C:V_C + KD], ACT.Silu).then_inc(csil_ready, 1)
            act.wait_ge(angles_ready, 1)
            do(sinT, ang[1], ACT.Sin).then_inc(tables_ready, 1)
            do(cosT, ang[2], ACT.Sin).then_inc(tables_ready, 1)
            for t in range(NT):
                act.wait_ge(x_loaded[t], 16)
                if t >= 2:
                    act.wait_ge(ssq_ready, t - 1)
                do(sq[:, t % 2], x_in[:, t], ACT.Square, accum_out=ssq[:, t:t + 1]).then_inc(ssq_ready, 1)
            act.wait_ge(ssq_ready, NT)
            do(std[:, :], ssq[:, :], ACT.Sqrt, bias=bias[:, 0:1], scale=1.0 / D).then_inc(std_ready, 1)
            act.wait_ge(gain1_ready, 1)
            for t in range(NT):
                act.wait_ge(xT_ready, t + 1)
                for k in range(KD // 2):
                    last = do(hT[:, k, t * P:(t + 1) * P], pair[2 + t % 2][:, k * P:(k + 1) * P], ACT.Identity,
                              bias=modc[:, k:k + 1], scale=gain1[:, k:k + 1])
                last.then_inc(hT_act, 1)

            def store(i):
                mms, dst, func, load = groups[i]
                act.wait_ge(proj_ready, i + 1)
                if i == G_LAT:
                    act.wait_ge(normed, N_JOBS)
                src = bank(i % 4)
                if i == G_AB:
                    src = src[:, 0:NT * 8]
                do(dst, src, func).then_inc(proj_stored, 1)

            def silu_conv(j):
                act.wait_ge(conv_ready, j + 1)
                do(qkvT[:, j], conv[:, j % 2], ACT.Silu).then_inc(conv_stored, 1)

            for j in range(12):
                store(2 * j)
                store(2 * j + 1)
                if j >= 1:
                    silu_conv(j - 1)
            store(24)
            silu_conv(11)
            for i in range(25, G_LAT):
                store(i)
            act.wait_ge(proj_stored, G_AB + 1)
            ab3 = ab[:, :].rearrange("p (t n) -> p t n", n=8)
            do(beta[:, :].rearrange("p (t h) -> p t h", h=H), ab3[:, :, H:2 * H], ACT.Sigmoid).then_inc(ab_parts, 1)
            act.wait_ge(ab_parts, 2)
            do(gtmp[:, 32:64], gtmp[:, 0:32], ACT.Exp, scale=-1.0).then_inc(ab_parts, 1)
            do(negrate[:, 0:H], heads[:, 0:H], ACT.Exp).then_inc(ab_parts, 1)
            act.wait_ge(ab_parts, 4)
            do(gtmp[:, 32:64], gtmp[:, 32:64], ACT.Ln, bias=bias[:, 2:3]).then_inc(ab_parts, 1)
            act.wait_ge(conv_stored, 12)
            for idx, (n, k, of, src) in enumerate(norm_tiles):
                if idx >= 2:
                    act.wait_ge(sumsq_ready, idx - 1)
                do(sq[:, idx % 2], src, ACT.Square).then_inc(squares_ready, 1)
            act.wait_ge(sumsq_ready, len(norm_tiles))
            for a, b, scale, eps in ((0, 1, 1.0 / QR, 0), (1, 2, 1.0 / KVR, 0), (2, 6, float(P), 1), (6, 10, 1.0, 0)):
                do(ncol[:, a * NT:b * NT], bank(4)[:, a * NT:b * NT], ACT.Sqrt, bias=bias[:, eps:eps + 1], scale=scale)\
                    .then_inc(ncol_ready, 1)
            NG = NT * H
            act.wait_ge(gcum_ready, 1)
            act.wait_ge(ekd_in, 1)
            do(egc[:, :], bank(4)[:, 0:NG], ACT.Exp).then_inc(gexp_ready, 1)
            do(egl[:, :], bank(4)[:, 2 * NG:4 * NG], ACT.Exp).then_inc(gexp_ready, 1)
            act.wait_ge(ekd_in, 3)
            do(ekd[:, :], ekd[:, :], ACT.Exp).then_inc(gexp_ready, 1)
            for i in range(G_LAT, N_GROUPS):
                store(i)
            for a in range(N_ST + 2):
                if a < N_ST:
                    keys = (score_tiles[a][0] + 1) * P
                    act.wait_ge(negmax_ready, a + 1)
                    if a >= 2:
                        act.wait_ge(probT_ready, a - 1)
                    do(prob[:, a % 2, 0:keys], pair[a % 2][:, 0:keys], ACT.Exp, bias=negmax[:, a:a + 1], scale=MLA_SCALE,
                       accum_out=rowsum[:, a:a + 1]).then_inc(exp_ready, 1)
                if 1 <= a <= N_ST:
                    b = a - 1
                    keys = (score_tiles[b][0] + 1) * P
                    act.wait_ge(probT_ready, b + 1)
                    if b >= 2:
                        act.wait_ge(pv_ready, b - 1)
                    do(probT[:, b % 2, 0:keys], pair[2][:, 0:keys], ACT.Copy).then_inc(probT_stored, 1)
                if a >= 2:
                    b = a - 2
                    i, h = score_tiles[b]
                    act.wait_ge(pv_ready, b + 1)
                    do(oT_mla[:, h, i * P:(i + 1) * P], bank(6 + b % 2)[:, 0:P], ACT.Copy).then_inc(o_stored, 1)
            gdn_act(act)
            out_act(act)
            moe_act(act)

        @block.vector
        def _(dve):
            v = nc.vector
            steps = [0]

            def then(ins):
                steps[0] += 1
                ins.then_inc(vector_step, 1)
                dve.wait_ge(vector_step, steps[0])

            dve.wait_ge(setup_loaded, N_SETUP)
            dve.wait_ge(vecT_ready, 1)
            v.tensor_copy(vec[:, :], bank(0)[:, 0:NVEC]).then_inc(vec_ready, 1)
            then(v.tensor_copy(ang[1], pos))
            then(v.tensor_scalar(ang[1], ang[1], consts[:, C_INVF:C_INVF + 1], None, ALU.mult))
            then(v.tensor_scalar(ang[3], ang[1], 1.0 / TWO_PI, ROUND, ALU.mult, ALU.add))
            then(v.tensor_scalar(ang[3], ang[3], ROUND, None, ALU.subtract))
            c1 = 6.28125
            c2 = float(np.array([np.float32(TWO_PI - c1).view(np.uint32) & np.uint32(0xFFFFF000)], np.uint32).view(np.float32)[0])
            c3 = float(np.float32(TWO_PI - c1 - c2))
            for part in (c1, c2, c3):
                then(v.scalar_tensor_tensor(ang[1], ang[3], -part, ang[1], ALU.mult, ALU.add))
            then(v.tensor_scalar(ang[2], ang[1], float(np.pi / 2), None, ALU.add))
            then(v.tensor_scalar(ang[3], ang[2], float(np.pi), -float(TWO_PI), ALU.is_gt, ALU.mult))
            then(v.tensor_tensor(ang[2], ang[2], ang[3], ALU.add))
            top = 3.1415925
            then(v.tensor_scalar(ang[1], ang[1], top, -top, ALU.min, ALU.max))
            v.tensor_scalar(ang[2], ang[2], top, -top, ALU.min, ALU.max).then_inc(angles_ready, 1)
            dve.wait_ge(std_ready, 1)
            then(v.reciprocal(rstd[:, :], std[:, :]))
            for t in range(NT):
                v.tensor_scalar(x_in[:, t], x_in[:, t], rstd[:, t:t + 1], None, ALU.mult).then_inc(xn_ready, 1)
            dve.wait_ge(vec_ready, 1)
            dve.wait_ge(mod_ready, 4)
            then(v.tensor_tensor(modc[:, 0:16], bank(1)[:, 0:16], vec[:, V_ADAB:V_ADAB + 16], ALU.add))
            v.scalar_tensor_tensor(gain1[:, :], modc[:, 8:16], 1.0, vec[:, V_N1:V_N1 + KD], ALU.add, ALU.mult)\
                .then_inc(gain1_ready, 1)
            dve.wait_ge(gain1_ready, 1)
            for t in range(NT):
                dve.wait_ge(xT_ready, t + 1)
                for k in range(KD // 2, KD):
                    last = v.tensor_scalar(hT[:, k, t * P:(t + 1) * P], pair[2 + t % 2][:, k * P:(k + 1) * P],
                                           gain1[:, k:k + 1], modc[:, k:k + 1], ALU.mult, ALU.add)
                last.then_inc(hT_dve, 1)
            dve.wait_ge(tables_ready, 2)
            then(v.tensor_scalar(sinT, sinT, consts[:, C_SIGN:C_SIGN + 1], None, ALU.mult))
            for j in range(12):
                dve.wait_ge(proj_stored, 2 * j + 2)
                if j >= 2:
                    dve.wait_ge(conv_stored, j - 1)
                x, y = qkvT[:, j], conv[:, j % 2]
                tap = [vec[:, V_CONV + 12 * i + j:V_CONV + 12 * i + j + 1] for i in range(4)]
                then(v.tensor_scalar(y, x, tap[3], None, ALU.mult))
                for back in (1, 2, 3):
                    ins = v.scalar_tensor_tensor(y[:, back:S], x[:, 0:S - back], tap[3 - back], y[:, back:S], ALU.mult, ALU.add)
                    if back < 3:
                        then(ins)
                ins.then_inc(conv_ready, 1)
            R2 = ROPE // 2
            dve.wait_ge(ring_loaded[L_CKV % 3], 16 * (L_CKV // 3 + 1))
            src = slot(L_CKV)[:, :, KVR:KVR + ROPE]
            for half in range(2):
                at = half * ROPE
                v.tensor_copy(wkpe[:, :, at:at + ROPE], src)
                v.tensor_copy(wkpe[:, :, P + at:P + at + R2], src[:, :, R2:ROPE])
                ins = v.tensor_copy(wkpe[:, :, P + at + R2:P + at + ROPE], src[:, :, 0:R2])
            ins.then_inc(wpe_ready, 1)
            ab3 = ab[:, :].rearrange("p (t n) -> p t n", n=8)
            y, e, m = (gtmp[:, 32 * i:32 * i + 32] for i in range(3))
            y3 = m.rearrange("p (t h) -> p t h", h=H)
            dve.wait_ge(proj_stored, G_AB + 1)
            then(v.tensor_tensor(y3, ab3[:, :, 0:H], heads[:, H:2 * H].unsqueeze(1).broadcast_to([P, NT, H]), ALU.add))
            dve.wait_ge(ab_parts, 1)
            v.scalar_tensor_tensor(y, m, -1.0, m, ALU.mult, ALU.max).then_inc(ab_parts, 1)
            dve.wait_ge(ab_parts, 5)
            then(v.scalar_tensor_tensor(e, m, 0.0, e, ALU.max, ALU.add))
            then(v.tensor_scalar(negrate[:, H:2 * H], negrate[:, 0:H], -1.0, None, ALU.mult))
            v.tensor_tensor(g[:, :].rearrange("p (t h) -> p t h", h=H), e.rearrange("p (t h) -> p t h", h=H),
                            negrate[:, H:2 * H].unsqueeze(1).broadcast_to([P, NT, H]), ALU.mult).then_inc(g_ready, 1)
            dve.wait_ge(ncol_ready, 4)
            then(v.reciprocal(rcol[:, :], ncol[:, :]))

            def make_diag(n):
                if n >= 2:
                    dve.wait_ge(spread_ready, n - 1)
                if n == 0:
                    dve.wait_ge(proj_ready, G_AB)
                v.tensor_tensor(diag[:, n % 2].rearrange("p (t c) -> p t c", t=NT),
                                ident.unsqueeze(1).broadcast_to([P, NT, P]),
                                rcol[:, n * NT:(n + 1) * NT].unsqueeze(2).broadcast_to([P, NT, P]),
                                ALU.mult).then_inc(diag_ready, 1)

            make_diag(0)
            for n, (srcs, gain) in enumerate(norm_jobs):
                if n + 1 < N_JOBS:
                    make_diag(n + 1)
                dve.wait_ge(spread_ready, n + 1)
                for k, x in enumerate(srcs):
                    if gain is None:
                        ins = v.tensor_tensor(x, x, pair[2 + n % 2][:, :], ALU.mult)
                    else:
                        ins = v.scalar_tensor_tensor(x, x, vec[:, gain + k:gain + k + 1], pair[2 + n % 2][:, :],
                                                     ALU.mult, ALU.mult)
                ins.then_inc(normed, 1)
            dve.wait_ge(ring_loaded[L_WQ % 3], 16 * (L_WQ // 3 + 1))
            for k in range(KQ):
                src = slot(L_WQ)[:, k].rearrange("p (h n) -> p h n", h=H)
                dst = wqpe[:, k].rearrange("p (s h n) -> p s h n", s=2, h=H)
                v.tensor_copy(dst[:, 0], src[:, :, NOPE:QH])
                v.tensor_copy(dst[:, 1, :, 0:R2], src[:, :, NOPE + R2:QH])
                ins = v.tensor_copy(dst[:, 1, :, R2:ROPE], src[:, :, NOPE:NOPE + R2])
            ins.then_inc(wpe_ready, 1)
            NG = NT * H
            dve.wait_ge(gcum_ready, 1)
            v.tensor_copy(gcs[:, :], bank(4)[:, 0:NG]).then_inc(ekd_in, 1)
            dve.wait_ge(gexp_ready, 2)
            dve.wait_ge(ekd_in, 1)
            v.tensor_tensor(ekd[:, :], bank(4)[:, NG:2 * NG], gcs[:, :], ALU.subtract).then_inc(ekd_in, 2)
            def rope(x, sw):
                then(v.tensor_tensor(x, x, cosT, ALU.mult))
                then(v.tensor_tensor(sw, sw, sinT, ALU.mult))
                v.tensor_tensor(x, x, sw, ALU.add).then_inc(roped, 1)

            rope(kpe, kpe_sw)
            for i in range(2):
                dve.wait_ge(proj_stored, G_LAT + 2 * H + 4 * (i + 1))
                rope(qpe[:, i], qpe_sw[:, i])
            for a in range(N_ST + 1):
                if a < N_ST:
                    keys = (score_tiles[a][0] + 1) * P
                    dve.wait_ge(scores_ready, a + 1)
                    then(v.memset(pair[a % 2][0:CHUNK, keys - CHUNK:keys], NEG))
                    then(v.tensor_reduce(rowmax[:, a:a + 1], pair[a % 2][:, 0:keys], AX.X, ALU.max))
                    v.tensor_scalar(negmax[:, a:a + 1], rowmax[:, a:a + 1], -MLA_SCALE, None, ALU.mult)\
                        .then_inc(negmax_ready, 1)
                if a >= 1:
                    b = a - 1
                    keys = (score_tiles[b][0] + 1) * P
                    dve.wait_ge(exp_ready, b + 1)
                    then(v.reciprocal(rowinv[:, b:b + 1], rowsum[:, b:b + 1]))
                    v.tensor_scalar(prob[:, b % 2, 0:keys], prob[:, b % 2, 0:keys], rowinv[:, b:b + 1], None, ALU.mult)\
                        .then_inc(prob_ready, 1)
            gdn_dve(dve, then)
            out_dve(dve, then)
            moe_dve(dve, then)


_INS = ["x", "c", "positions", "ada_w", "ada_b", "norm1_w", "w_in", "q_a_norm_w", "wq_b", "kv_a_norm_w", "wkv_b",
        "gdn_conv_w", "gdn_a_log", "gdn_dt_bias", "gdn_norm_w", "w_out", "norm2_w", "router_w", "router_bias",
        "exp_w_gate", "exp_w_up", "exp_w_down", "sh_w_gate", "sh_w_up", "sh_w_down", "final_norm_w"]


def kernel(**inputs):
    import concourse.bacc as bacc
    from concourse.bass_utils import run_bass_kernel_spmd

    nc = bacc.Bacc("TRN2", target_bir_lowering=False, num_devices=1)
    arrays = {name: np.ascontiguousarray(inputs[name]) for name in _INS}
    arrays["shape_constants"] = shape_constants()
    arrays["late_constants"] = late_constants()
    aps = {name: nc.dram_tensor(f"in_{name}", a.shape, mybir.dt.from_np(a.dtype), kind="ExternalInput").ap()
           for name, a in arrays.items()}
    out = nc.dram_tensor("out_0", (1, S, D), F32, kind="ExternalOutput").ap()
    hybrid_block(nc, aps, out)
    r = run_bass_kernel_spmd(nc, [{f"in_{name}": a for name, a in arrays.items()}], core_ids=[0])
    return r.results[0]["out_0"]
```
